# Optimizing a Trainium2 kernel written in Bass

```python
import numpy as np
import jax
import jax.numpy as jnp
from jax import lax

D_MODEL = 1024
BATCH = 1
SEQ = 256
DEPTH = 1

HEAD_DIM = 64
NSA_HEADS = 8
NSA_KV_HEADS = 2
NSA_GROUP = NSA_HEADS // NSA_KV_HEADS
MOBA_HEADS = 8
D_NSA = NSA_HEADS * HEAD_DIM
D_NSA_KV = NSA_KV_HEADS * HEAD_DIM
D_MOBA = MOBA_HEADS * HEAD_DIM
D_MIX = D_NSA + D_MOBA
N_NSA_BRANCHES = 3
ROPE_THETA = 500000.0
ROPE_DIM = HEAD_DIM // 4
CMP_BLOCK = 32
CMP_STRIDE = 16
CMP_HIDDEN = 4 * HEAD_DIM
SEL_BLOCK = 64
SEL_TOPK = 16
WINDOW = 512
NSA_Q_CHUNK = 64
MOBA_BLOCK = 256
MOBA_TOPK = 3
MOBA_Q_CHUNK = 32
LN_EPS = 1e-5
DEEPNORM_ALPHA = (2.0 * DEPTH) ** 0.25
DEEPNORM_BETA = (8.0 * DEPTH) ** -0.25
NEG_BIG = -1e30
POS_BIG = 1e30

PROJ_SIZES = (D_NSA, D_NSA_KV, D_NSA_KV, D_NSA_KV, D_NSA_KV, D_NSA_KV, D_NSA_KV,
              N_NSA_BRANCHES * NSA_HEADS, D_NSA, D_MOBA, D_MOBA, D_MOBA, D_MOBA)
VALUE_SLOTS = (2, 4, 6, 11)
D_PROJ = sum(PROJ_SIZES)
PROJ_OFFSETS = tuple(int(o) for o in np.cumsum(PROJ_SIZES)[:-1])

kernel_name = "hymba_nsa_moba_deepnorm_block"

def rope_tables(T):
    inv_freq = ROPE_THETA ** (-jnp.arange(0, ROPE_DIM, 2, dtype=jnp.float32) / ROPE_DIM)
    ang = jnp.arange(T, dtype=jnp.float32)[:, None] * inv_freq[None, :]
    return jnp.cos(ang), jnp.sin(ang)

def partial_rope(x, cos, sin):
    half = ROPE_DIM // 2
    xr = x[..., :ROPE_DIM].astype(jnp.float32)
    x1, x2 = xr[..., :half], xr[..., half:]
    c = cos[None, :, None, :]
    s = sin[None, :, None, :]
    rot = jnp.concatenate([x1 * c - x2 * s, x2 * c + x1 * s], axis=-1).astype(x.dtype)
    return jnp.concatenate([rot, x[..., ROPE_DIM:]], axis=-1)

def masked_softmax(s, mask):
    s = jnp.where(mask, s.astype(jnp.float32), NEG_BIG)
    m = jnp.max(s, axis=-1, keepdims=True)
    e = jnp.where(mask, jnp.exp(s - m), 0.0)
    d = jnp.sum(e, axis=-1, keepdims=True)
    return e / jnp.where(d > 0, d, 1.0)

def layer_norm(h, gain, bias):
    hf = h.astype(jnp.float32)
    mu = jnp.mean(hf, axis=-1, keepdims=True)
    var = jnp.mean(jnp.square(hf - mu), axis=-1, keepdims=True)
    y = (hf - mu) * lax.rsqrt(var + LN_EPS) * gain.astype(jnp.float32) + bias.astype(jnp.float32)
    return y.astype(h.dtype)

def gather_blocks(blocks, idx):
    return jax.vmap(jax.vmap(lambda bl, ix: bl[ix]))(blocks, idx)

def compress(kv, pos, w1, b1, w2):
    B, T, G, d = kv.shape
    n_per = CMP_BLOCK // CMP_STRIDE
    nc0 = T // CMP_STRIDE
    nc = nc0 - n_per + 1
    ch = kv.reshape(B, nc0, CMP_STRIDE, G, d)
    blocks = jnp.concatenate([ch[:, i:i + nc] for i in range(n_per)], axis=2)
    blocks = blocks + pos[None, None, :, None, :]
    flat = blocks.transpose(0, 3, 1, 2, 4).reshape(B, G, nc, CMP_BLOCK * d)
    return jax.nn.silu(flat @ w1 + b1) @ w2

def nsa_attention(q, k_cmp, v_cmp, k_slc, v_slc, k_win, v_win, gate_logits,
                  cmp_pos_k, cmp_w1_k, cmp_b1_k, cmp_w2_k,
                  cmp_pos_v, cmp_w1_v, cmp_b1_v, cmp_w2_v, cos, sin):
    B, T = q.shape[0], q.shape[1]
    G, R, d = NSA_KV_HEADS, NSA_GROUP, HEAD_DIM
    scale = d ** -0.5

    def to_groups(a):
        return a.reshape(B, T, G, R, d).transpose(0, 2, 3, 1, 4)

    q_raw = to_groups(q)
    q_rot = to_groups(partial_rope(q, cos, sin))

    kc = compress(k_cmp, cmp_pos_k, cmp_w1_k, cmp_b1_k, cmp_w2_k)
    vc = compress(v_cmp, cmp_pos_v, cmp_w1_v, cmp_b1_v, cmp_w2_v)
    nc = kc.shape[2]
    ns = T // SEL_BLOCK
    ks = partial_rope(k_slc, cos, sin).transpose(0, 2, 1, 3).reshape(B, G, ns, SEL_BLOCK, d)
    vs = v_slc.transpose(0, 2, 1, 3).reshape(B, G, ns, SEL_BLOCK, d)
    pad = ((0, 0), (0, 0), (WINDOW, 0), (0, 0))
    kw = jnp.pad(partial_rope(k_win, cos, sin).transpose(0, 2, 1, 3), pad)
    vw = jnp.pad(v_win.transpose(0, 2, 1, 3), pad)
    gates = jax.nn.sigmoid(gate_logits.astype(jnp.float32)).reshape(B, T, G, R, N_NSA_BRANCHES)
    gates = gates.transpose(0, 2, 3, 1, 4)

    c_start = jnp.arange(nc)[:, None] * CMP_STRIDE
    s_start = jnp.arange(ns)[None, :] * SEL_BLOCK
    overlap = ((c_start < s_start + SEL_BLOCK) & (c_start + CMP_BLOCK > s_start)).astype(jnp.float32)
    cmp_end = jnp.arange(nc) * CMP_STRIDE + CMP_BLOCK - 1
    n_sel = min(SEL_TOPK, ns)
    Qc = NSA_Q_CHUNK
    blk_ids = jnp.arange(ns)

    def chunk(c):
        s0 = c * Qc
        t = s0 + jnp.arange(Qc)
        qr = lax.dynamic_slice_in_dim(q_rot, s0, Qc, axis=3)
        qn = lax.dynamic_slice_in_dim(q_raw, s0, Qc, axis=3)
        g = lax.dynamic_slice_in_dim(gates, s0, Qc, axis=3)

        sc = jnp.einsum('bghqd,bgcd->bghqc', qn, kc) * scale
        pc = masked_softmax(sc, cmp_end[None, :] <= t[:, None])
        o_cmp = jnp.einsum('bghqc,bgcd->bghqd', pc.astype(vc.dtype), vc)

        imp = jnp.einsum('bghqc,cs->bgqs', pc, overlap)
        qblk = (t // SEL_BLOCK)[:, None]
        forced = (blk_ids[None, :] == 0) | (blk_ids[None, :] == qblk) | (blk_ids[None, :] == qblk - 1)
        imp = jnp.where(forced, POS_BIG, jnp.where(blk_ids[None, :] > qblk, NEG_BIG, imp))
        _, idx = lax.top_k(imp, n_sel)
        gk = gather_blocks(ks, idx)
        gv = gather_blocks(vs, idx)
        kpos = idx[..., None] * SEL_BLOCK + jnp.arange(SEL_BLOCK)
        ms = (kpos <= t[None, None, :, None, None]).reshape(B, G, 1, Qc, n_sel * SEL_BLOCK)
        ss = jnp.einsum('bghqd,bgqnld->bghqnl', qr, gk) * scale
        ps = masked_softmax(ss.reshape(B, G, R, Qc, n_sel * SEL_BLOCK), ms)
        ps = ps.reshape(ss.shape).astype(gv.dtype)
        o_slc = jnp.einsum('bghqnl,bgqnld->bghqd', ps, gv)

        kwin = lax.dynamic_slice_in_dim(kw, s0, Qc + WINDOW, axis=2)
        vwin = lax.dynamic_slice_in_dim(vw, s0, Qc + WINDOW, axis=2)
        kpos_w = (s0 - WINDOW + jnp.arange(Qc + WINDOW))[None, :]
        mw = (kpos_w <= t[:, None]) & (kpos_w > t[:, None] - WINDOW) & (kpos_w >= 0)
        sw = jnp.einsum('bghqd,bgkd->bghqk', qr, kwin) * scale
        pw = masked_softmax(sw, mw).astype(vwin.dtype)
        o_win = jnp.einsum('bghqk,bgkd->bghqd', pw, vwin)

        o = g[..., 0:1] * o_cmp + g[..., 1:2] * o_slc + g[..., 2:3] * o_win
        return o.astype(q.dtype)

    out = lax.map(chunk, jnp.arange(T // Qc))
    return out.transpose(1, 0, 4, 2, 3, 5).reshape(B, T, D_NSA)

def moba_attention(q, k, v, cos, sin):
    B, T = q.shape[0], q.shape[1]
    H, d, MB = MOBA_HEADS, HEAD_DIM, MOBA_BLOCK
    scale = d ** -0.5
    nb = max(-(-T // MB), 2)
    Tp = nb * MB
    pad = ((0, 0), (0, Tp - T), (0, 0), (0, 0))
    qp = jnp.pad(partial_rope(q, cos, sin), pad).transpose(0, 2, 1, 3)
    kp = jnp.pad(partial_rope(k, cos, sin), pad).transpose(0, 2, 1, 3)
    vp = jnp.pad(v, pad).transpose(0, 2, 1, 3)
    kb = kp.reshape(B, H, nb, MB, d)
    vb = vp.reshape(B, H, nb, MB, d)
    kmean = jnp.mean(kb.astype(jnp.float32), axis=3)
    k_top = min(MOBA_TOPK, nb - 1)
    Qc = MOBA_Q_CHUNK
    blk_ids = jnp.arange(nb)

    def chunk(c):
        s0 = c * Qc
        own = s0 // MB
        t = s0 + jnp.arange(Qc)
        qc = lax.dynamic_slice_in_dim(qp, s0, Qc, axis=2)
        sg = jnp.einsum('bhqd,bhnd->bhqn', qc.astype(jnp.float32), kmean)
        sg = jnp.where(blk_ids < own, sg, NEG_BIG)
        _, idx = lax.top_k(sg, k_top)
        valid = idx < own
        gk = gather_blocks(kb, idx)
        gv = gather_blocks(vb, idx)
        sp = jnp.einsum('bhqd,bhqnld->bhqnl', qc, gk).reshape(B, H, Qc, k_top * MB)
        mp = jnp.broadcast_to(valid[..., None], (B, H, Qc, k_top, MB)).reshape(B, H, Qc, k_top * MB)
        ko = lax.dynamic_slice_in_dim(kp, own * MB, MB, axis=2)
        vo = lax.dynamic_slice_in_dim(vp, own * MB, MB, axis=2)
        so = jnp.einsum('bhqd,bhld->bhql', qc, ko)
        mo = jnp.broadcast_to((own * MB + jnp.arange(MB))[None, :] <= t[:, None], so.shape)
        s = jnp.concatenate([sp, so], axis=-1) * scale
        m = jnp.concatenate([mp, mo], axis=-1)
        p = masked_softmax(s, m).astype(v.dtype)
        pp = p[..., :k_top * MB].reshape(B, H, Qc, k_top, MB)
        o = jnp.einsum('bhqnl,bhqnld->bhqd', pp, gv) + jnp.einsum('bhql,bhld->bhqd', p[..., k_top * MB:], vo)
        return o.astype(q.dtype)

    out = lax.map(chunk, jnp.arange(Tp // Qc))
    return out.transpose(1, 0, 3, 2, 4).reshape(B, Tp, D_MOBA)[:, :T]

def hybrid_layer(x, w_in, cmp_pos_k, cmp_w1_k, cmp_b1_k, cmp_w2_k,
                 cmp_pos_v, cmp_w1_v, cmp_b1_v, cmp_w2_v, w_out, ln_gain, ln_bias, cos, sin):
    B, T, _ = x.shape
    proj = x @ w_in
    (nsa_q, nsa_kc, nsa_vc, nsa_ks, nsa_vs, nsa_kw, nsa_vw, nsa_g, nsa_z,
     moba_q, moba_k, moba_v, moba_z) = jnp.split(proj, list(PROJ_OFFSETS), axis=-1)

    def heads(a, h):
        return a.reshape(B, T, h, HEAD_DIM)

    y_nsa = nsa_attention(heads(nsa_q, NSA_HEADS),
                          heads(nsa_kc, NSA_KV_HEADS), heads(nsa_vc, NSA_KV_HEADS),
                          heads(nsa_ks, NSA_KV_HEADS), heads(nsa_vs, NSA_KV_HEADS),
                          heads(nsa_kw, NSA_KV_HEADS), heads(nsa_vw, NSA_KV_HEADS),
                          nsa_g, cmp_pos_k, cmp_w1_k, cmp_b1_k, cmp_w2_k,
                          cmp_pos_v, cmp_w1_v, cmp_b1_v, cmp_w2_v, cos, sin)
    y_moba = moba_attention(heads(moba_q, MOBA_HEADS), heads(moba_k, MOBA_HEADS),
                            heads(moba_v, MOBA_HEADS), cos, sin)
    y = jnp.concatenate([y_nsa * jax.nn.silu(nsa_z), y_moba * jax.nn.silu(moba_z)], axis=-1)
    sub = y @ w_out
    return layer_norm(DEEPNORM_ALPHA * x + sub, ln_gain, ln_bias)

def setup_inputs(seed: int = 0) -> dict:
    key = jax.random.key(seed)
    ks = jax.random.split(key, 13)
    f32 = jnp.float32
    col_scale = np.ones((D_PROJ,), np.float32)
    starts = (0,) + PROJ_OFFSETS
    for slot in VALUE_SLOTS:
        col_scale[starts[slot]:starts[slot] + PROJ_SIZES[slot]] = DEEPNORM_BETA
    fan_c = CMP_BLOCK * HEAD_DIM
    x = jax.random.normal(ks[0], (BATCH, SEQ, D_MODEL), f32)
    w_in = jax.random.normal(ks[1], (DEPTH, D_MODEL, D_PROJ), f32) * (D_MODEL ** -0.5) * jnp.asarray(col_scale)
    cmp_pos_k = 0.02 * jax.random.normal(ks[2], (DEPTH, CMP_BLOCK, HEAD_DIM), f32)
    cmp_w1_k = jax.random.normal(ks[3], (DEPTH, fan_c, CMP_HIDDEN), f32) * fan_c ** -0.5
    cmp_b1_k = 0.01 * jax.random.normal(ks[4], (DEPTH, CMP_HIDDEN), f32)
    cmp_w2_k = jax.random.normal(ks[5], (DEPTH, CMP_HIDDEN, HEAD_DIM), f32) * CMP_HIDDEN ** -0.5
    cmp_pos_v = 0.02 * jax.random.normal(ks[6], (DEPTH, CMP_BLOCK, HEAD_DIM), f32)
    cmp_w1_v = jax.random.normal(ks[7], (DEPTH, fan_c, CMP_HIDDEN), f32) * fan_c ** -0.5
    cmp_b1_v = 0.01 * jax.random.normal(ks[8], (DEPTH, CMP_HIDDEN), f32)
    cmp_w2_v = jax.random.normal(ks[9], (DEPTH, CMP_HIDDEN, HEAD_DIM), f32) * CMP_HIDDEN ** -0.5
    w_out = jax.random.normal(ks[10], (DEPTH, D_MIX, D_MODEL), f32) * (D_MIX ** -0.5) * DEEPNORM_BETA
    ln_gain = 1.0 + 0.02 * jax.random.normal(ks[11], (DEPTH, D_MODEL), f32)
    ln_bias = 0.02 * jax.random.normal(ks[12], (DEPTH, D_MODEL), f32)
    return {"x": x, "w_in": w_in,
            "cmp_pos_k": cmp_pos_k, "cmp_w1_k": cmp_w1_k, "cmp_b1_k": cmp_b1_k, "cmp_w2_k": cmp_w2_k,
            "cmp_pos_v": cmp_pos_v, "cmp_w1_v": cmp_w1_v, "cmp_b1_v": cmp_b1_v, "cmp_w2_v": cmp_w2_v,
            "w_out": w_out, "ln_gain": ln_gain, "ln_bias": ln_bias}

def reference(x, w_in, cmp_pos_k, cmp_w1_k, cmp_b1_k, cmp_w2_k,
              cmp_pos_v, cmp_w1_v, cmp_b1_v, cmp_w2_v, w_out, ln_gain, ln_bias):
    cos, sin = rope_tables(x.shape[1])
    h = x
    for layer in range(DEPTH):
        h = hybrid_layer(h, w_in[layer],
                         cmp_pos_k[layer], cmp_w1_k[layer], cmp_b1_k[layer], cmp_w2_k[layer],
                         cmp_pos_v[layer], cmp_w1_v[layer], cmp_b1_v[layer], cmp_w2_v[layer],
                         w_out[layer], ln_gain[layer], ln_bias[layer], cos, sin)
    return h


_drawn_inputs = setup_inputs


def setup_inputs(seed=0):
    import zlib

    import numpy as np

    out = dict(_drawn_inputs(seed))
    spreads = {}
    factors = {'cmp_pos_k': 8.0,
     'cmp_w1_k': 8.0,
     'cmp_b1_k': 44.281,
     'cmp_w2_k': 8.0,
     'cmp_pos_v': 8.0,
     'cmp_w1_v': 3.129,
     'cmp_b1_v': 32.125,
     'cmp_w2_v': 2.698,
     'ln_gain': 7.998,
     'ln_bias': 8.169}
    for name, (base, spread) in spreads.items():
        noise = np.random.default_rng([zlib.crc32(name.encode()), seed]).standard_normal(out[name].shape)
        drawn = base * np.exp(spread * noise) if base else spread * noise
        out[name] = jnp.asarray(drawn.astype(out[name].dtype))
    for name, factor in factors.items():
        out[name] = (out[name] * factor).astype(out[name].dtype)
    return out
```

```python
import numpy as np
import concourse.bass as bass
from concourse import mybir
from contextlib import ExitStack

P = 128
SEQ, D_MODEL, HEAD_DIM = 256, 1024, 64
TT = SEQ // P
KT = D_MODEL // P
GROUPS, REPS = 2, 4
D_NSA, D_MOBA = 512, 512
KV = GROUPS * HEAD_DIM
CH = 512
GATES = 3 * GROUPS * REPS
NARROW = 2 * KV + GATES
ROPE, HALF = HEAD_DIM // 4, HEAD_DIM // 8
ROPE_THETA = 500000.0
CMP_BLOCK, CMP_STRIDE, CMP_HIDDEN = 32, 16, 256
NCMP = SEQ // CMP_STRIDE - 1
CPAD = 16
CKT = CMP_BLOCK * HEAD_DIM // P
LN_EPS = 1e-5
ALPHA = 2.0 ** 0.25
NEG = -1e30
SCALE = HEAD_DIM ** -0.5

C_KV, C_NQ, C_NV, C_MK, C_MQ, C_MV, C_NZ, C_MZ, C_OA, C_OB = range(10)
STEPS = 4 * 8
UNIT0 = 12
UNITS = 18
RAW, HL, PIECE = 5, 3, 4 * CH

PIECES = ([("x", 0, 0)] + [("w", c, k) for c in (C_KV, C_NQ) for k in (0, 1)]
          + [("fk", 0, 0), ("fk", 0, 1)] + [("w", c, k) for c in (C_NV, C_MK) for k in (0, 1)]
          + [("fv", 1, 0), ("fv", 1, 1)]
          + [("w", c, k) for c in (C_MQ, C_MV, C_NZ, C_MZ, C_OA, C_OB) for k in (0, 1)]
          + [("res", 0, 0), ("gb", 0, 0)])

TURNS = ([("kv0", "act"), ("kv1", "act"), ("qraw0", "act"), ("hk", "dve"), ("qraw1", "act"),
          ("qrot0", "act"), ("qrot1", "act")]
         + [("hv", "dve")]
         + [("p0", "dve"), ("hT", "dve")]
         + [("p1", "dve"), ("kcvc", "dve")]
         + [("p2", "dve"), ("cs", "dve")]
         + [("p3", "dve"), ("mk0", "act")]
         + [("p4", "dve"), ("cp", "act")]
         + [("p5", "dve"), ("mk1", "act")]
         + [("p6", "dve"), ("mq0", "act")]
         + [("p7", "dve"), ("oc0", "dve")]
         + [("p8", "dve"), ("oc1", "dve")]
         + [("p9", "dve"), ("mq1", "act")]
         + [("p10", "dve"), ("p11", "dve"), ("p12", "dve"), ("p13", "dve"), ("p14", "dve")]
         + [("p15", "dve"), ("yn0", "dve")]
         + [("p16", "dve"), ("p17", "dve")]
         + [("yn1", "dve")]
         + [("ym0", "dve"), ("ym1", "dve")])
TURN_AT = {name: n for n, (name, _) in enumerate(TURNS)}


def turn_reads(name):
    n = TURN_AT[name]
    engine = TURNS[n][1]
    return engine, sum(e == engine for _, e in TURNS[:n + 1])


def unit_of(i):
    return i // 3, i % 3


def width(c):
    return NARROW if c == C_NV else CH


K_IDENT, K_SEL, K_CAUSAL, K_CMASK, K_CVALID, K_BLOCK, K_COS, K_SIN = range(8)
K_SIZES = [P, P, P, TT * P, TT * CPAD, GROUPS * REPS, TT * ROPE, TT * ROPE]
K_AT = [sum(K_SIZES[:n]) for n in range(len(K_SIZES) + 1)]


def constants():
    k = np.zeros((P, K_AT[-1]), np.float32)
    at = lambda n: k[:, K_AT[n]:K_AT[n + 1]]
    row = np.arange(P)
    at(K_IDENT)[:] = np.eye(P)
    at(K_SEL)[:] = (row[:, None] % 32 == row[None, :] % 32)
    at(K_CAUSAL)[:] = np.where(row[None, :] > row[:, None], NEG, 0.0)
    c = np.arange(CPAD)
    for t in range(TT):
        ok = (c[None, :] * CMP_STRIDE + CMP_BLOCK - 1 <= (t * P + row)[:, None]) & (c[None, :] < NCMP)
        at(K_CVALID)[:, t * CPAD:(t + 1) * CPAD] = ok
        at(K_CMASK)[:, t * P:(t + 1) * P] = np.tile(np.where(ok, 0.0, NEG), (1, P // CPAD))
    at(K_BLOCK)[:] = 0.5 * (row[:, None] // CPAD == np.arange(P // CPAD)[None, :])
    inv = np.float32(ROPE_THETA) ** (-np.arange(0, ROPE, 2, dtype=np.float32) / np.float32(ROPE))
    ang = np.arange(SEQ, dtype=np.float32)[:, None] * inv[None, :].astype(np.float32)
    cos, sin = np.cos(ang), np.sin(ang)
    for t in range(TT):
        rows = slice(t * P, (t + 1) * P)
        at(K_COS)[:, t * ROPE:(t + 1) * ROPE] = np.concatenate([cos[rows], cos[rows]], 1)
        at(K_SIN)[:, t * ROPE:(t + 1) * ROPE] = np.concatenate([-sin[rows], sin[rows]], 1)
    return k


def build(nc, xT, w_full, w_nv, w1, kmat, pos, b1, w2k, w2v, x_res, gain_bias, out):
    f32, f32r, bf16 = mybir.dt.float32, mybir.dt.float32r, mybir.dt.bfloat16
    ALU, ACT, AX = mybir.AluOpType, mybir.ActivationFunctionType, mybir.AxisListType
    ctx = ExitStack()
    with ctx:
        def sb(name, shape, dt=f32):
            return ctx.enter_context(nc.sbuf_tensor(name, shape, dt))

        def ps(name):
            return ctx.enter_context(nc.psum_tensor(name, [P, CH], f32))

        def sem(name):
            return ctx.enter_context(nc.semaphore(name))

        raw = sb("raw", [P, RAW, PIECE])
        w_hi = sb("w_hi", [P, HL, 4, CH], f32r)
        w_lo = sb("w_lo", [P, HL, 4, CH], f32r)
        x_hi = sb("x_hi", [P, KT, SEQ], f32r)
        x_lo = sb("x_lo", [P, KT, SEQ], f32r)
        k_sb = sb("k_sb", [P, K_AT[-1]])
        ident_bf = sb("ident_bf", [P, P], bf16)
        causal_bf = sb("causal_bf", [P, 2, P], bf16)
        cmask_bf = sb("cmask_bf", [P, TT, P], bf16)
        pos_sb = sb("pos_sb", [P, 2, 2, CKT])
        b1_sb = sb("b1_sb", [1, 2, CMP_HIDDEN])
        ones_sb = sb("ones_sb", [1, P])
        w2k_sb = sb("w2k_sb", [P, 2, P])
        w2v_sb = sb("w2v_sb", [P, 2, HEAD_DIM])
        keys_tok = sb("keys_tok", [P, TT, CH])
        q_tok = sb("q_tok", [P, TT, CH])
        swapped = sb("swapped", [P, 8, ROPE])
        qa_T = sb("qa_T", [P, REPS, SEQ])
        qrot_T = sb("qrot_T", [P, REPS, SEQ])
        kB_nsa = sb("kB_nsa", [P, 2, GROUPS, SEQ])
        kB_moba = sb("kB_moba", [P, 4, 2, SEQ])
        kvc_T = sb("kvc_T", [P, 2, SEQ])
        cmp_in = sb("cmp_in", [P, 2, CKT, 2 * CPAD])
        hid_parts = sb("hid_parts", [P, 2, CMP_HIDDEN])
        hid = sb("hid", [P, 2, 2, P])
        kc_B = sb("kc_B", [P, GROUPS * CPAD])
        vc_B = sb("vc_B", [P, D_NSA])
        cmp_p = sb("cmp_p", [P, TT, P])
        cmp_stat = sb("cmp_stat", [P, 3, TT, 8])
        cmp_pT = sb("cmp_pT", [P, TT, P])
        v_nsa = sb("v_nsa", [P, TT, 2, KV])
        v_moba = sb("v_moba", [P, TT, D_MOBA])
        gates = sb("gates", [P, 2, GATES])
        silu_z = sb("silu_z", [P, 2, D_MODEL])
        y = sb("y", [P, 2, D_MODEL])
        probs = sb("probs", [P, 2, CH])
        probs_T = sb("probs_T", [P, 2, CH])
        neg_max = sb("neg_max", [P, 2, 4])
        row_sum = sb("row_sum", [P, 6, 8])
        weight = sb("weight", [P, 8])
        weight2 = sb("weight2", [P, 8])
        scaled = sb("scaled", [P, CH])
        y_hi = sb("y_hi", [P, KT, SEQ], f32r)
        y_lo = sb("y_lo", [P, KT, SEQ], f32r)
        stats = sb("stats", [P, TT, 2, 6])
        moments = sb("moments", [P, TT, 2])
        rstd = sb("rstd", [P, TT, 3])

        acc = [ps(f"acc{n}") for n in range(2)]
        scores = [ps(f"scores{n}") for n in range(2)]
        turn = [ps(f"turn{n}") for n in range(2)]
        heads = [ps(f"heads{n}") for n in range(2)]

        raw_in = [sem(f"raw_in{n}") for n in range(RAW)]
        k_in, pos_in, b1_in, w2k_in, w2v_in = (sem(n) for n in ("k_in", "pos_in", "b1_in", "w2k_in", "w2v_in"))
        x_hi_ok, x_lo_ok = sem("x_hi_ok"), sem("x_lo_ok")
        hi_ok, lo_ok = sem("hi_ok"), sem("lo_ok")
        bf_ok = sem("bf_ok")
        zero_ok = sem("zero_ok")
        group_done = sem("group_done")
        acc_read = sem("acc_read")
        z_tanh, z_read = sem("z_tanh"), sem("z_read")
        gates_tanh, gates_ok = sem("gates_tanh"), sem("gates_ok")
        rope_a, rope_ok = sem("rope_a"), sem("rope_ok")
        turn_full = sem("turn_full")
        turn_act, turn_dve = sem("turn_act"), sem("turn_dve")
        turn_read = {"act": turn_act, "dve": turn_dve}
        packed = sem("packed")
        hid_read = sem("hid_read")
        hid_tanh = sem("hid_tanh")
        scores_ok, max_ok, probs_ok = sem("scores_ok"), sem("max_ok"), sem("probs_ok")
        heads_ok, heads_read = sem("heads_ok"), sem("heads_read")
        norm = sem("norm")
        cmp_shift, cmp_exp, cmp_pok = sem("cmp_shift"), sem("cmp_exp"), sem("cmp_pok")
        y_ok = sem("y_ok")
        yT_hi, = (sem("yT_hi"),)
        out_ok = sem("out_ok")
        mom_ok, eps_ok, rstd_ok, fin_ok = sem("mom_ok"), sem("eps_ok"), sem("rstd_ok"), sem("fin_ok")
        stored = [sem(f"stored{n}") for n in range(2 * TT)]

        const = lambda n: k_sb[:, K_AT[n]:K_AT[n + 1]]
        ident = const(K_IDENT)
        out_bank = {(0, 0): acc[0], (0, 1): scores[0], (1, 0): acc[1], (1, 1): scores[1]}
        res = PIECES.index(("res", 0, 0))
        gb = PIECES.index(("gb", 0, 0))
        x_tok = raw[:, res % RAW, :].rearrange("p (s n) -> p s n", s=2)
        gain = raw[:, gb % RAW, 0:D_MODEL]
        bias = raw[:, gb % RAW, D_MODEL:2 * D_MODEL]

        def wait_piece(eng, piece):
            n = PIECES.index(piece)
            eng.wait_ge(raw_in[n % RAW], 16 * (n // RAW + 1))

        def wait_turn_free(eng, name):
            n = TURN_AT[name]
            if n >= 2:
                engine, count = turn_reads(TURNS[n - 2][0])
                eng.wait_ge(turn_read[engine], count)

        def wait_turn(eng, name):
            eng.wait_ge(turn_full, TURN_AT[name] + 1)

        def turn_bank(name):
            return turn[TURN_AT[name] % 2]

        block = ctx.enter_context(nc.Block())

        @block.sync
        def _(sp):
            for n, (kind, c, k) in enumerate(PIECES):
                if n >= RAW:
                    old, oc, ok = PIECES[n - RAW]
                    if old == "x":
                        sp.wait_ge(x_lo_ok, 2)
                    elif old == "w":
                        sp.wait_ge(lo_ok, 4 * oc + 2 * ok + 2)
                    elif ok == 0:
                        sp.wait_ge(hid_read, oc + 1)
                    else:
                        wait_turn(sp, ("hk", "hv")[oc])
                dst = raw[:, n % RAW, :]
                if kind == "x":
                    src = xT
                elif kind == "w" and c == C_NV:
                    dst, src = raw[:, n % RAW, 0:4 * NARROW], w_nv[k]
                elif kind == "w":
                    src = w_full[2 * (c - (c > C_NV)) + k]
                elif kind == "res":
                    src = x_res
                elif kind == "gb":
                    src = gain_bias.partition_broadcast(P)
                else:
                    src = w1[c, k]
                sp.dma_start(dst, src).then_inc(raw_in[n % RAW], 16)
            for t in range(TT):
                for n in range(2):
                    sp.wait_ge(fin_ok, 2 * t + n + 1)
                    sp.dma_start(out[t * P:(t + 1) * P, n * CH:(n + 1) * CH],
                                 y[:, 1 - t, n * CH:(n + 1) * CH]).then_inc(stored[2 * t + n], 16)
            for s in stored:
                sp.wait_ge(s, 16)

        @block.gpsimd
        def _(pool):
            pool.memset(kB_nsa[:, :, :, :], 0.0).then_inc(zero_ok, 1)
            pool.memset(kc_B[:, :], 0.0).then_inc(zero_ok, 1)
            pool.memset(cmp_in[:, :, :, :], 0.0).then_inc(zero_ok, 1)
            pool.memset(ones_sb[:, :], 1.0).then_inc(zero_ok, 1)
            pool.memset(kB_moba[:, :, :, :], 0.0).then_inc(zero_ok, 1)
            pool.wait_ge(k_in, 16)
            for n, (c, t) in enumerate((c, t) for c in (C_KV, C_NQ, C_MK, C_MQ) for t in range(TT)):
                pool.wait_ge(acc_read, 2 * c + t + 1)
                if c == C_NQ:
                    wait_turn(pool, f"qraw{t}")
                tok = keys_tok if c in (C_KV, C_MK) else q_tok
                at = 2 * KV if c == C_KV else 0
                nh = (CH - at) // HEAD_DIM
                v = tok[:, t, at:CH].rearrange("p (h d) -> p h d", d=HEAD_DIM)
                cos = const(K_COS)[:, t * ROPE:(t + 1) * ROPE].unsqueeze(1).broadcast_to((P, nh, ROPE))
                sin = const(K_SIN)[:, t * ROPE:(t + 1) * ROPE].unsqueeze(1).broadcast_to((P, nh, ROPE))
                part = swapped[:, 0:nh, :]
                if n:
                    pool.wait_ge(rope_ok, n)
                pool.tensor_tensor(part[:, :, 0:HALF], v[:, :, HALF:ROPE], sin[:, :, 0:HALF], ALU.mult).then_inc(rope_a, 1)
                pool.tensor_tensor(part[:, :, HALF:ROPE], v[:, :, 0:HALF], sin[:, :, HALF:ROPE], ALU.mult).then_inc(rope_a, 1)
                pool.wait_ge(rope_a, 3 * n + 2)
                pool.tensor_tensor(v[:, :, 0:ROPE], v[:, :, 0:ROPE], cos, ALU.mult).then_inc(rope_a, 1)
                pool.wait_ge(rope_a, 3 * n + 3)
                pool.tensor_tensor(v[:, :, 0:ROPE], v[:, :, 0:ROPE], part, ALU.add).then_inc(rope_ok, 1)
            pool.memset(rstd[:, :, 2:3], -0.5).then_inc(eps_ok, 1)
            for t in range(TT):
                pool.wait_ge(mom_ok, t + 1)
                pool.tensor_scalar(rstd[:, t, 0:1], moments[:, t, 1:2], LN_EPS, None, ALU.add).then_inc(eps_ok, 1)
                pool.wait_ge(eps_ok, t + 2)
                pool.tensor_tensor(rstd[:, t, 1:2], rstd[:, t, 0:1], rstd[:, t, 2:3], ALU.pow).then_inc(rstd_ok, 1)

        @block.scalar
        def _(act):
            act.dma_start(k_sb[:, :], kmat).then_inc(k_in, 16)
            act.dma_start(pos_sb[:, :, :, :], pos).then_inc(pos_in, 16)
            act.dma_start(b1_sb[:, :, :], b1).then_inc(b1_in, 16)
            act.dma_start(w2k_sb[:, :, :], w2k).then_inc(w2k_in, 16)
            act.dma_start(w2v_sb[:, :, :], w2v).then_inc(w2v_in, 16)

            def split_x(j):
                wait_piece(act, ("x", 0, 0))
                act.activation(x_hi[:, 4 * j:4 * j + 4, :].rearrange("p k t -> p (k t)"),
                               raw[:, 0, j * PIECE // 2:(j + 1) * PIECE // 2], ACT.Copy).then_inc(x_hi_ok, 1)

            def split(u):
                c, k, j = u // 4, u % 4 // 2, u % 2
                piece = 2 * c + k
                wait_piece(act, ("w", c, k))
                if piece >= HL:
                    act.wait_ge(group_done, last_use(piece - HL))
                w = width(c)
                n = PIECES.index(("w", c, k))
                src = raw[:, n % RAW, 2 * j * w:2 * (j + 1) * w].rearrange("p (k n) -> p k n", k=2)
                act.activation(w_hi[:, piece % HL, 2 * j:2 * j + 2, 0:w], src, ACT.Copy).then_inc(hi_ok, 1)

            def copy_group(c, t):
                act.wait_ge(group_done, 4 * c + 2 * t + 2)
                src = acc[t]
                if c == C_KV:
                    act.activation(keys_tok[:, t, :], src[:, :], ACT.Copy).then_inc(acc_read, 1)
                elif c == C_MK:
                    wait_turn(act, "kv1")
                    act.activation(keys_tok[:, t, :], src[:, :], ACT.Copy).then_inc(acc_read, 1)
                elif c == C_NQ:
                    act.activation(q_tok[:, t, :], src[:, :], ACT.Copy, scale=SCALE).then_inc(acc_read, 1)
                elif c == C_MQ:
                    wait_turn(act, "qrot1")
                    act.activation(q_tok[:, t, :], src[:, :], ACT.Copy, scale=SCALE).then_inc(acc_read, 1)
                elif c == C_NV:
                    act.activation(gates[:, 1 - t, :], src[:, 2 * KV:NARROW], ACT.Tanh, scale=0.5).then_inc(gates_tanh, 1)
                    act.activation(v_nsa[:, t, :, :], src[:, 0:2 * KV].rearrange("p (b n) -> p b n", b=2), ACT.Copy).then_inc(acc_read, 1)
                elif c == C_MV:
                    act.activation(v_moba[:, t, :], src[:, :], ACT.Copy).then_inc(acc_read, 1)
                else:
                    at = (c - C_NZ) * CH
                    act.activation(silu_z[:, 1 - t, at:at + CH], src[:, :], ACT.Tanh, scale=0.5).then_inc(z_tanh, 1)

            def exps(i):
                g, kind = unit_of(i)
                act.wait_ge(max_ok, i + 1)
                if i >= 2:
                    wait_turn(act, f"p{i - 2}")
                n, w = (2, 2 * P) if kind < 2 else (4, P)
                at = 2 * kind
                for h in range(n):
                    last = act.activation(probs[:, i % 2, h * w:(h + 1) * w], scores[i % 2][:, h * w:(h + 1) * w], ACT.Exp,
                                          bias=neg_max[:, i % 2, h:h + 1],
                                          accum_out=row_sum[:, g, at + h:at + h + 1])
                last.then_inc(probs_ok, 1)

            def keys_out(name, t):
                wait_turn(act, name)
                b = turn_bank(name)[:, :].rearrange("p (m t) -> p m t", m=4)
                tok = slice(t * P, (t + 1) * P)
                if name[:2] == "kv":
                    if t == 0:
                        act.wait_ge(zero_ok, 1)
                    act.activation(kvc_T[:, :, tok], b[:, 0:2, :], ACT.Copy)
                    act.activation(kB_nsa[0:64, :, 0, tok], b[0:64, 2:4, :], ACT.Copy)
                    act.activation(kB_nsa[64:P, :, 1, tok], b[64:P, 2:4, :], ACT.Copy).then_inc(turn_act, 1)
                else:
                    if t == 0:
                        act.wait_ge(zero_ok, 5)
                    act.activation(kB_moba[0:64, :, 0, tok], b[0:64, :, :], ACT.Copy)
                    act.activation(kB_moba[64:P, :, 1, tok], b[64:P, :, :], ACT.Copy).then_inc(turn_act, 1)

            def queries_out(name, dst, t):
                wait_turn(act, name)
                act.activation(dst[:, :, t * P:(t + 1) * P], turn_bank(name)[:, :].rearrange("p (m t) -> p m t", m=4),
                               ACT.Copy).then_inc(turn_act, 1)

            def y_hi_out(name, half, t):
                wait_turn(act, name)
                act.activation(y_hi[:, 4 * half:4 * half + 4, t * P:(t + 1) * P],
                               turn_bank(name)[:, :].rearrange("p (m t) -> p m t", m=4), ACT.Copy).then_inc(yT_hi, 1)

            split_x(0)
            split(0)
            split_x(1)
            for u in range(1, 4):
                split(u)
            for s in range(STEPS):
                c, t, k = s // 4, s % 4 // 2, s % 2
                i = s - UNIT0
                if k == 0 and s:
                    copy_group((s - 1) // 4, (s - 1) % 4 // 2)
                if 1 <= i <= UNITS:
                    exps(i - 1)
                if s == 5:
                    keys_out("kv0", 0)
                if s == 6:
                    keys_out("kv1", 1)
                if s == 7:
                    queries_out("qraw0", qa_T, 0)
                if s == 9:
                    queries_out("qraw1", qa_T, 1)
                if s == 10:
                    queries_out("qrot0", qrot_T, 0)
                if s == 12:
                    queries_out("qrot1", qrot_T, 1)
                if s == 14:
                    wait_turn(act, "hT")
                    act.activation(hid[:, :, :, :], turn_bank("hT")[:, :].rearrange("p (a b n) -> p a b n", a=2, b=2),
                                   ACT.Tanh, scale=0.5).then_inc(hid_tanh, 1)
                if s == 16:
                    act.wait_ge(cmp_shift, 1)
                    act.activation(cmp_p[:, :, :], cmp_p[:, :, :], ACT.Exp).then_inc(cmp_exp, 1)
                if s == 17:
                    keys_out("mk0", 0)
                if s == 18:
                    wait_turn(act, "cp")
                    act.activation(cmp_pT[:, :, :], turn_bank("cp")[:, 0:TT * P].rearrange("p (t n) -> p t n", t=TT),
                                   ACT.Copy).then_inc(turn_act, 1)
                if s == 19:
                    keys_out("mk1", 1)
                if s == 20:
                    queries_out("mq0", qa_T, 0)
                if s == 23:
                    queries_out("mq1", qa_T, 1)
                if s == 29:
                    y_hi_out("yn0", 0, 0)
                if s == 31:
                    y_hi_out("yn1", 0, 1)
                for u in splits_in(s):
                    split(u)
            copy_group(C_MZ, 1)
            split(4 * C_OB)
            split(4 * C_OB + 1)
            y_hi_out("ym0", 1, 0)
            split(4 * C_OB + 2)
            split(4 * C_OB + 3)
            y_hi_out("ym1", 1, 1)

        @block.vector
        def _(dve):
            chain = [0]

            def link(instruction):
                chain[0] += 1
                instruction.then_inc(norm, 1)
                dve.wait_ge(norm, chain[0])

            def split_x(j):
                dve.wait_ge(x_hi_ok, j + 1)
                dve.tensor_tensor(x_lo[:, 4 * j:4 * j + 4, :].rearrange("p k t -> p (k t)"),
                                  raw[:, 0, j * PIECE // 2:(j + 1) * PIECE // 2],
                                  x_hi[:, 4 * j:4 * j + 4, :].bitcast(f32).rearrange("p k t -> p (k t)"),
                                  ALU.subtract).then_inc(x_lo_ok, 1)

            def split(u):
                c, k, j = u // 4, u % 4 // 2, u % 2
                piece = 2 * c + k
                w = width(c)
                n = PIECES.index(("w", c, k))
                dve.wait_ge(hi_ok, u + 1)
                src = raw[:, n % RAW, 2 * j * w:2 * (j + 1) * w].rearrange("p (k n) -> p k n", k=2)
                at = (slice(None), piece % HL, slice(2 * j, 2 * j + 2), slice(0, w))
                dve.tensor_tensor(w_lo[at], src, w_hi[at].bitcast(f32), ALU.subtract).then_inc(lo_ok, 1)

            def silu_out(c, t):
                dve.wait_ge(z_tanh, 2 * (c - C_NZ) + t + 1)
                part = silu_z[:, 1 - t, (c - C_NZ) * CH:(c - C_NZ + 1) * CH]
                dve.scalar_tensor_tensor(part, part, 1.0, acc[t][:, :], ALU.add, ALU.mult).then_inc(z_read, 1)

            def maxima(i):
                dve.wait_ge(scores_ok, i + 1)
                if i >= 2:
                    dve.wait_ge(probs_ok, i - 1)
                n = 2 if unit_of(i)[1] < 2 else 4
                dve.tensor_reduce(neg_max[:, i % 2, 0:n], scores[i % 2][:, :].rearrange("p (n k) -> p n k", n=n),
                                  AX.X, ALU.max, negate=True).then_inc(max_ok, 1)

            def probs_out(i):
                wait_turn(dve, f"p{i}")
                if i >= 2:
                    dve.wait_ge(heads_ok, i - 1)
                dve.tensor_copy(probs_T[:, i % 2, :], turn_bank(f"p{i}")[:, :]).then_inc(turn_dve, 1)

            updates = [0]

            def updated(instruction):
                updates[0] += 1
                instruction.then_inc(y_ok, 1)
                dve.wait_ge(y_ok, updates[0])

            def heads_out(g):
                dve.wait_ge(heads_ok, 3 * g + 3)
                dve.wait_ge(probs_ok, 3 * g + 3)
                link(dve.reciprocal(weight[:, :], row_sum[:, g, :]))
                w = weight
                if g < 4:
                    branch, r = 1 + g // 2, 2 * (g % 2)
                    at = branch * 8 + 2 * r
                    link(dve.tensor_tensor(weight2[:, :].rearrange("p (s n) -> p s n", s=2),
                                           weight[:, :].rearrange("p (s n) -> p s n", s=2),
                                           gates[:, :, at:at + 4], ALU.mult))
                    w = weight2
                    cols = slice(r * 2 * HEAD_DIM, (r + 2) * 2 * HEAD_DIM)
                else:
                    cols = slice(D_NSA + (g - 4) * 256, D_NSA + (g - 3) * 256)
                src = heads[g % 2][:, :].rearrange("p (h d) -> p h d", d=HEAD_DIM)
                wide = w[:, :].unsqueeze(2).broadcast_to((P, 8, HEAD_DIM))
                if g in (2, 3):
                    dve.tensor_tensor(scaled[:, :].rearrange("p (h d) -> p h d", d=HEAD_DIM), src, wide,
                                      ALU.mult).then_inc(heads_read, 1)
                    dve.wait_ge(heads_read, g + 1)
                    updated(dve.tensor_tensor(y[:, :, cols], y[:, :, cols],
                                              scaled[:, :].rearrange("p (s n) -> p s n", s=2), ALU.add))
                else:
                    for s in range(2):
                        last = dve.tensor_tensor(y[:, s, cols].rearrange("p (h d) -> p h d", d=HEAD_DIM),
                                                 src[:, 4 * s:4 * s + 4, :], wide[:, 4 * s:4 * s + 4, :], ALU.mult)
                    last.then_inc(heads_read, 1)
                    dve.wait_ge(heads_read, g + 1)

            def gate_y(half, t):
                dve.wait_ge(z_read, 2 * half + t + 1)
                part = y[:, 1 - t, half * CH:(half + 1) * CH]
                updated(dve.scalar_tensor_tensor(part, part, 0.5, silu_z[:, 1 - t, half * CH:(half + 1) * CH],
                                                 ALU.mult, ALU.mult))

            def y_lo_out(name, half, t, n):
                dve.wait_ge(yT_hi, n)
                at = (slice(None), slice(4 * half, 4 * half + 4), slice(t * P, (t + 1) * P))
                dve.tensor_tensor(y_lo[at], turn_bank(name)[:, :].rearrange("p (m t) -> p m t", m=4),
                                  y_hi[at].bitcast(f32), ALU.subtract).then_inc(turn_dve, 1)

            def pack(kind):
                for g in range(GROUPS):
                    rows = slice(64 * g, 64 * g + 64)
                    src = kvc_T[rows, kind, :].rearrange("p (c w) -> p c w", w=CMP_STRIDE)
                    for parity in range(2):
                        for half in range(2):
                            n = CKT // 2
                            v = src[:, half:half + NCMP, parity::2].rearrange("p c k -> p k c")
                            term = pos_sb[rows, kind, parity, half * n:(half + 1) * n].unsqueeze(2).broadcast_to((64, n, NCMP))
                            dve.tensor_tensor(cmp_in[64 * parity:64 * parity + 64, kind, half * n:(half + 1) * n,
                                                     g * CPAD:g * CPAD + NCMP], v, term, ALU.add).then_inc(packed, 1)

            split_x(0)
            split(0)
            split_x(1)
            for u in range(1, 4):
                split(u)
            dve.wait_ge(k_in, 16)
            dve.tensor_copy(ident_bf[:, :], ident)
            dve.tensor_copy(causal_bf[:, 0, :], const(K_CAUSAL))
            dve.tensor_copy(causal_bf[:, 1, :], const(K_CAUSAL))
            dve.tensor_copy(cmask_bf[:, :, :], const(K_CMASK).rearrange("p (t n) -> p t n", t=TT)).then_inc(bf_ok, 1)
            for s in range(STEPS):
                c, t, k = s // 4, s % 4 // 2, s % 2
                i = s - UNIT0
                if k == 0 and (s - 1) // 4 >= C_NZ:
                    silu_out((s - 1) // 4, (s - 1) % 4 // 2)
                if 1 <= i <= UNITS:
                    maxima(i - 1)
                if 2 <= i < UNITS + 2:
                    probs_out(i - 2)
                if i >= 3 and i % 3 == 2 and i // 3 <= 6:
                    heads_out((i - 5) // 3)
                if s == 7:
                    dve.wait_ge(turn_act, 2)
                    dve.wait_ge(pos_in, 16)
                    dve.wait_ge(zero_ok, 3)
                    pack(0)
                if s == 8:
                    wait_turn(dve, "hk")
                    dve.tensor_copy(hid_parts[:, 0, :], turn_bank("hk")[:, 0:CMP_HIDDEN]).then_inc(turn_dve, 1)
                    pack(1)
                if s == 12:
                    dve.wait_ge(gates_tanh, 2)
                    dve.tensor_scalar(gates[:, :, :], gates[:, :, :], 1.0, 0.5, ALU.add, ALU.mult).then_inc(gates_ok, 1)
                if s == 13:
                    wait_turn(dve, "hv")
                    dve.tensor_copy(hid_parts[:, 1, :], turn_bank("hv")[:, 0:CMP_HIDDEN]).then_inc(turn_dve, 1)
                if s == 14:
                    dve.wait_ge(hid_tanh, 1)
                    dve.scalar_tensor_tensor(hid[:, :, :, :].rearrange("p a b n -> p (a b n)"),
                                             hid[:, :, :, :].rearrange("p a b n -> p (a b n)"), 1.0,
                                             turn_bank("hT")[:, :], ALU.add, ALU.mult).then_inc(turn_dve, 1)
                if s == 15:
                    wait_turn(dve, "kcvc")
                    b = turn_bank("kcvc")
                    dve.wait_ge(zero_ok, 2)
                    dve.tensor_scalar(kc_B[0:64, 0:CPAD], b[0:64, 0:CPAD], 0.5, None, ALU.mult)
                    dve.tensor_scalar(kc_B[64:P, CPAD:2 * CPAD], b[64:P, CPAD:2 * CPAD], 0.5, None, ALU.mult)
                    dve.tensor_tensor(vc_B[:, :].rearrange("p (n d) -> p n d", d=HEAD_DIM),
                                      b[:, 64:P].unsqueeze(1).broadcast_to((P, 8, HEAD_DIM)),
                                      const(K_BLOCK).unsqueeze(2).broadcast_to((P, 8, HEAD_DIM)), ALU.mult).then_inc(turn_dve, 1)
                if s == 16:
                    wait_turn(dve, "cs")
                    b = turn_bank("cs")[:, 0:TT * P].rearrange("p (n c) -> p n c", c=CPAD)
                    stat = lambda n: cmp_stat[:, n, :, :].rearrange("p t h -> p (t h)")
                    wide = lambda n: stat(n).unsqueeze(2).broadcast_to((P, TT * 8, CPAD))
                    e = cmp_p[:, :, :].rearrange("p t (h c) -> p (t h) c", c=CPAD)
                    link(dve.tensor_reduce(stat(0), b, AX.X, ALU.max, negate=True))
                    dve.tensor_tensor(e, b, wide(0), ALU.add).then_inc(turn_dve, 1)
                    dve.wait_ge(turn_dve, turn_reads("cs")[1])
                    dve.tensor_copy(cmp_stat[:, 1, :, :], cmp_stat[:, 0, :, :]).then_inc(cmp_shift, 1)
                    dve.wait_ge(cmp_shift, 1)
                if s == 17:
                    dve.wait_ge(cmp_exp, 1)
                    for t2 in range(TT):
                        e2 = cmp_p[:, t2, :].rearrange("p (h c) -> p h c", c=CPAD)
                        last = dve.tensor_tensor(e2, e2, const(K_CVALID)[:, t2 * CPAD:(t2 + 1) * CPAD].unsqueeze(1)
                                                 .broadcast_to((P, 8, CPAD)), ALU.mult)
                    link(last)
                    link(dve.tensor_reduce(stat(1), e, AX.X, ALU.add))
                    link(dve.tensor_scalar(stat(1), stat(1), 0.5, None, ALU.max))
                    link(dve.reciprocal(stat(2), stat(1)))
                    for t2 in range(TT):
                        last = dve.tensor_tensor(cmp_stat[:, 2, t2, :], cmp_stat[:, 2, t2, :], gates[:, 1 - t2, 0:8], ALU.mult)
                    link(last)
                    dve.tensor_tensor(e, e, wide(2), ALU.mult).then_inc(cmp_pok, 1)
                if s in (21, 22):
                    t2 = s - 21
                    wait_turn(dve, f"oc{t2}")
                    updates_before = dve.tensor_tensor(y[:, 1 - t2, 0:D_NSA], y[:, 1 - t2, 0:D_NSA],
                                                       turn_bank(f"oc{t2}")[:, :], ALU.add)
                    updates_before.then_inc(turn_dve, 1)
                    dve.wait_ge(turn_dve, turn_reads(f"oc{t2}")[1])
                if s in (27, 29):
                    gate_y(0, (s - 27) // 2)
                if s in (29, 31):
                    y_lo_out(f"yn{(s - 29) // 2}", 0, (s - 29) // 2, 1 + (s - 29) // 2)
                for u in splits_in(s):
                    split(u)
            silu_out(C_MZ, 1)
            heads_out(5)
            for t in range(TT):
                gate_y(1, t)
            split(4 * C_OB)
            split(4 * C_OB + 1)
            y_lo_out("ym0", 1, 0, 3)
            split(4 * C_OB + 2)
            split(4 * C_OB + 3)
            y_lo_out("ym1", 1, 1, 4)
            wait_piece(dve, ("res", 0, 0))
            wait_piece(dve, ("gb", 0, 0))
            for t in range(TT):
                for n in range(2):
                    part = y[:, 1 - t, n * CH:(n + 1) * CH]
                    dve.wait_ge(out_ok, 2 * t + n + 1)
                    link(dve.scalar_tensor_tensor(part, x_tok[:, 1 - t, n * CH:(n + 1) * CH], ALPHA,
                                                  out_bank[n, t][:, :], ALU.mult, ALU.add))
                    link(dve.bn_stats(stats[:, t, n, :], part))
                dve.bn_aggr(moments[:, t, :], stats[:, t, :, :].rearrange("p n s -> p (n s)")).then_inc(mom_ok, 1)
                dve.wait_ge(mom_ok, t + 1)
                for n in range(2):
                    part = y[:, 1 - t, n * CH:(n + 1) * CH]
                    link(dve.scalar_tensor_tensor(part, part, moments[:, t, 0:1], gain[:, n * CH:(n + 1) * CH],
                                                  ALU.subtract, ALU.mult))
                dve.wait_ge(rstd_ok, t + 1)
                for n in range(2):
                    part = y[:, 1 - t, n * CH:(n + 1) * CH]
                    dve.scalar_tensor_tensor(part, part, rstd[:, t, 1:2], bias[:, n * CH:(n + 1) * CH],
                                             ALU.mult, ALU.add).then_inc(fin_ok, 1)

        @block.tensor
        def _(pe):
            def project(s):
                c, t, k = s // 4, s % 4 // 2, s % 2
                n = 2 * c + t
                w = width(c)
                piece = (2 * c + k) % HL
                if k == 0 and n >= 2:
                    if n - 2 < 2 * C_NZ:
                        pe.wait_ge(acc_read, n - 1)
                    else:
                        pe.wait_ge(z_read, n - 1 - 2 * C_NZ)
                for j in range(4):
                    kt = 4 * k + j
                    if t == 0 and j % 2 == 0:
                        if s < 2 and j == 0:
                            pe.wait_ge(x_lo_ok, k + 1)
                        pe.wait_ge(lo_ok, 4 * c + 2 * k + j // 2 + 1)
                    tok = slice(t * P, (t + 1) * P)
                    pe.matmul(acc[t][:, 0:w], x_hi[:, kt, tok], w_hi[:, piece, j, 0:w], start=(kt == 0), stop=False)
                    pe.matmul(acc[t][:, 0:w], x_hi[:, kt, tok], w_lo[:, piece, j, 0:w], start=False, stop=False)
                    last = pe.matmul(acc[t][:, 0:w], x_lo[:, kt, tok], w_hi[:, piece, j, 0:w], start=False, stop=(kt == KT - 1))
                last.then_inc(group_done, 1)

            def transposes(name, blocks, n=4):
                wait_turn_free(pe, name)
                for m in range(n):
                    last = pe.transpose(turn_bank(name)[:, m * P:(m + 1) * P], blocks(m), ident)
                last.then_inc(turn_full, 1)

            def section_turn(name, tok, t, ropes):
                pe.wait_ge(rope_ok, ropes)
                transposes(name, lambda m: tok[:, t, m * P:(m + 1) * P])

            def unit_scores(i):
                g, kind = unit_of(i)
                if i >= 2:
                    pe.wait_ge(probs_ok, i - 1)
                bank = scores[i % 2]
                for pair in ((2 * (g % 2) + kind,) if kind < 2 else (2 * (g % 2), 2 * (g % 2) + 1)):
                    if g < 4:
                        q, keys = qrot_T, kB_nsa[:, g // 2, :, :]
                    else:
                        q, keys = qa_T, kB_moba[:, pair, :, :]
                    if kind < 2:
                        pe.matmul(bank[:, :], q[:, pair, P:SEQ], keys.rearrange("p h t -> p (h t)"), start=True, stop=False)
                        masked = bank[:, :].rearrange("p (h t) -> p h t", h=2)[:, :, P:SEQ]
                    else:
                        half = bank[:, (pair % 2) * 2 * P:(pair % 2 + 1) * 2 * P].rearrange("p (h t) -> p h t", h=2)
                        pe.matmul(half, q[:, pair, 0:P], keys[:, :, 0:P], start=True, stop=False)
                        masked = half
                    last = pe.matmul(masked, ident_bf[:, :], causal_bf[:, :, :], start=False, stop=True)
                last.then_inc(scores_ok, 1)

            def unit_turn(i):
                pe.wait_ge(probs_ok, i + 1)
                transposes(f"p{i}", lambda m: probs[:, i % 2, m * P:(m + 1) * P])

            def unit_heads(i):
                g, kind = unit_of(i)
                pe.wait_ge(turn_dve, turn_reads(f"p{i}")[1])
                if kind == 0 and g >= 2:
                    pe.wait_ge(heads_read, g - 1)
                for h in range(2 if kind < 2 else 4):
                    pair = 2 * (g % 2) + (kind if kind < 2 else h // 2)
                    side = h % 2
                    tiles = range(2) if kind < 2 else range(1)
                    for kt in tiles:
                        if g < 4:
                            v = v_nsa[:, kt, g // 2, side * HEAD_DIM:(side + 1) * HEAD_DIM]
                        else:
                            head = 2 * pair + side
                            v = v_moba[:, kt, head * HEAD_DIM:(head + 1) * HEAD_DIM]
                        at = (2 * kind + h) * HEAD_DIM
                        m = h * len(tiles) + kt
                        last = pe.matmul(heads[g % 2][:, at:at + HEAD_DIM], probs_T[:, i % 2, m * P:(m + 1) * P], v,
                                         start=(kt == 0), stop=(kt == tiles[-1]))
                last.then_inc(heads_ok, 1)

            def hidden(kind, name):
                wait_turn_free(pe, name)
                pe.wait_ge(packed, 8 * kind + 8)
                for i in range(CKT):
                    if i % 8 == 0:
                        n = PIECES.index((("fk", "fv")[kind], kind, i // 8))
                        wait_piece(pe, PIECES[n])
                    j = i % 4
                    w = raw[:, n % RAW, (i % 8) * CMP_HIDDEN:(i % 8 + 1) * CMP_HIDDEN]
                    last = pe.matmul(turn_bank(name)[32 * j:32 * j + 32, 0:CMP_HIDDEN], cmp_in[:, kind, i, :], w,
                                     start=(i < 4), stop=(i >= CKT - 4))
                    if i == CKT // 2 - 1:
                        last.then_inc(hid_read, 1)
                last.then_inc(turn_full, 1)

            pe.wait_ge(k_in, 16)
            for s in range(STEPS):
                i = s - UNIT0
                project(s)
                if 0 <= i < UNITS:
                    if i == 0:
                        pe.wait_ge(bf_ok, 1)
                        pe.wait_ge(turn_act, turn_reads("qrot1")[1])
                    if i == 12:
                        pe.wait_ge(turn_act, turn_reads("mq1")[1])
                    unit_scores(i)
                if s == 4:
                    section_turn("kv0", keys_tok, 0, 1)
                if s == 5:
                    section_turn("kv1", keys_tok, 1, 2)
                if s == 6:
                    pe.wait_ge(acc_read, 3)
                    transposes("qraw0", lambda m: q_tok[:, 0, m * P:(m + 1) * P])
                if s == 7:
                    hidden(0, "hk")
                if s == 8:
                    pe.wait_ge(acc_read, 4)
                    transposes("qraw1", lambda m: q_tok[:, 1, m * P:(m + 1) * P])
                if s == 9:
                    section_turn("qrot0", q_tok, 0, 3)
                if s == 11:
                    section_turn("qrot1", q_tok, 1, 4)
                if s == 12:
                    hidden(1, "hv")
                if 1 <= i <= UNITS:
                    unit_turn(i - 1)
                if 2 <= i <= UNITS + 1:
                    if i == 14:
                        pe.wait_ge(acc_read, 12)
                    unit_heads(i - 2)
                if s == 13:
                    wait_turn_free(pe, "hT")
                    pe.wait_ge(turn_dve, turn_reads("hv")[1])
                    pe.wait_ge(b1_in, 16)
                    pe.wait_ge(zero_ok, 4)
                    for kind in range(2):
                        for half in range(2):
                            cols = slice(half * P, (half + 1) * P)
                            dst = turn_bank("hT")[:, (2 * kind + half) * P:(2 * kind + half + 1) * P]
                            pe.matmul(dst, hid_parts[:, kind, cols], const(K_SEL), start=True, stop=False)
                            last = pe.matmul(dst, b1_sb[:, kind, cols], ones_sb[:, :], start=False, stop=True)
                    last.then_inc(turn_full, 1)
                if s == 14:
                    wait_turn_free(pe, "kcvc")
                    pe.wait_ge(turn_dve, turn_reads("hT")[1])
                    pe.wait_ge(w2k_in, 16)
                    pe.wait_ge(w2v_in, 16)
                    for half in range(2):
                        pe.matmul(turn_bank("kcvc")[:, 0:2 * CPAD], w2k_sb[:, half, :], hid[:, 0, half, 0:2 * CPAD],
                                  start=(half == 0), stop=(half == 1))
                    for half in range(2):
                        last = pe.matmul(turn_bank("kcvc")[:, 64:P], hid[:, 1, half, :], w2v_sb[:, half, :],
                                         start=(half == 0), stop=(half == 1))
                    last.then_inc(turn_full, 1)
                if s == 15:
                    wait_turn_free(pe, "cs")
                    pe.wait_ge(turn_dve, turn_reads("kcvc")[1])
                    pe.wait_ge(bf_ok, 1)
                    for t in range(TT):
                        for r in range(REPS):
                            at = t * P + r * 2 * CPAD
                            dst = turn_bank("cs")[:, at:at + 2 * CPAD]
                            pe.matmul(dst, qa_T[:, r, t * P:(t + 1) * P], kc_B[:, :], start=True, stop=False)
                            last = pe.matmul(dst, ident_bf[:, :], cmask_bf[:, t, r * 2 * CPAD:(r + 1) * 2 * CPAD],
                                             start=False, stop=True)
                    last.then_inc(turn_full, 1)
                if s == 16:
                    section_turn("mk0", keys_tok, 0, 5)
                if s == 17:
                    pe.wait_ge(cmp_pok, 1)
                    transposes("cp", lambda m: cmp_p[:, m, :], TT)
                if s in (20, 21):
                    t = s - 20
                    wait_turn_free(pe, f"oc{t}")
                    pe.wait_ge(turn_act, turn_reads("cp")[1])
                    pe.matmul(turn_bank(f"oc{t}")[:, :], cmp_pT[:, t, :], vc_B[:, :], start=True, stop=True).then_inc(turn_full, 1)
                if s == 18:
                    section_turn("mk1", keys_tok, 1, 6)
                if s == 19:
                    section_turn("mq0", q_tok, 0, 7)
                if s == 22:
                    section_turn("mq1", q_tok, 1, 8)
                if s in (28, 30):
                    t = (s - 28) // 2
                    pe.wait_ge(y_ok, 3 + t)
                    transposes(f"yn{t}", lambda m: y[:, 1 - t, m * P:(m + 1) * P])
            for e, (c, n, t) in enumerate([(C_OA, n, t) for n in range(2) for t in range(TT)]
                                          + [(C_OB, n, t) for t in range(TT) for n in range(2)]):
                if c == C_OA:
                    if n == 0 and t == 0:
                        pe.wait_ge(z_read, 3)
                        pe.wait_ge(probs_ok, UNITS)
                        pe.wait_ge(turn_dve, turn_reads("yn1")[1])
                    if n == 1 and t == 0:
                        pe.wait_ge(z_read, 4)
                elif n == 0:
                    pe.wait_ge(turn_dve, turn_reads(f"ym{t}")[1])
                first = 2 * (c - C_OA) + n
                for j in range(4):
                    if j % 2 == 0:
                        pe.wait_ge(lo_ok, 4 * C_OA + 2 * first + j // 2 + 1)
                    kt = 4 * (c - C_OA) + j
                    piece = (2 * C_OA + first) % HL
                    tok = slice(t * P, (t + 1) * P)
                    bank = out_bank[n, t]
                    pe.matmul(bank[:, :], y_hi[:, kt, tok], w_hi[:, piece, j, :], start=(kt == 0), stop=False)
                    pe.matmul(bank[:, :], y_hi[:, kt, tok], w_lo[:, piece, j, :], start=False, stop=False)
                    last = pe.matmul(bank[:, :], y_lo[:, kt, tok], w_hi[:, piece, j, :], start=False, stop=(kt == KT - 1))
                last.then_inc(group_done if c == C_OA else out_ok, 1)
                if e in (2, 3):
                    t = e - 2
                    pe.wait_ge(y_ok, 5 + t)
                    transposes(f"ym{t}", lambda m: y[:, 1 - t, D_NSA + m * P:D_NSA + (m + 1) * P])


def last_use(piece):
    c, k = piece // 2, piece % 2
    if c < C_OA:
        return 4 * c + 2 + k + 1
    return STEPS + 2 * k + 2


def splits_in(s):
    c = s // 4 + 1
    return {0: [4 * c], 1: [4 * c + 1], 2: [], 3: [4 * c + 2, 4 * c + 3]}[s % 4]


def kernel(x, w_in, cmp_pos_k, cmp_w1_k, cmp_b1_k, cmp_w2_k,
           cmp_pos_v, cmp_w1_v, cmp_b1_v, cmp_w2_v, w_out, ln_gain, ln_bias):
    import concourse.bacc as bacc
    from concourse.bass_utils import run_bass_kernel_spmd

    a = lambda v: np.asarray(v)
    x, w, wo = a(x)[0], a(w_in)[0], a(w_out)[0]
    sizes = [D_NSA] + [KV] * 6 + [GATES, D_NSA] + [D_MOBA] * 4
    at = np.cumsum([0] + sizes)
    q, kc, vc, ks, vs, kw, vw, ga, z, mq, mk, mv, mz = (w[:, at[n]:at[n + 1]] for n in range(13))

    def by_rep(m):
        return m.reshape(D_MODEL, GROUPS, REPS, HEAD_DIM).transpose(0, 2, 1, 3).reshape(D_MODEL, D_NSA)

    def pieces(m):
        return m.reshape(2, 4, P, -1).transpose(0, 2, 1, 3).reshape(2, P, -1)

    ga = ga.reshape(D_MODEL, GROUPS, REPS, 3).transpose(0, 3, 2, 1).reshape(D_MODEL, GATES)
    wo_nsa = wo[:D_NSA].reshape(GROUPS, REPS, HEAD_DIM, D_MODEL).transpose(1, 0, 2, 3).reshape(D_NSA, D_MODEL)

    def out_pieces(m):
        return m.reshape(4, P, 2, CH).transpose(2, 1, 0, 3).reshape(2, P, 4 * CH)

    chunks = [np.concatenate([kc, vc, ks, kw], 1), by_rep(q), mk, mq, mv, by_rep(z), mz]
    w_full = np.concatenate([pieces(m) for m in chunks] + [out_pieces(wo_nsa), out_pieces(wo[D_NSA:])])
    w_nv = pieces(np.concatenate([vs, vw, ga], 1))
    w1 = np.stack([a(m)[0].reshape(2, CKT // 2, P, CMP_HIDDEN).transpose(0, 2, 1, 3).reshape(2, P, PIECE)
                   for m in (cmp_w1_k, cmp_w1_v)])
    pos = np.stack([a(m)[0].reshape(CKT, 2, HEAD_DIM).transpose(2, 1, 0) for m in (cmp_pos_k, cmp_pos_v)], 1)
    pos = np.concatenate([pos, pos], 0)
    b1 = np.stack([a(cmp_b1_k)[0], a(cmp_b1_v)[0]])[None]
    w2k = a(cmp_w2_k)[0].reshape(2, P, HEAD_DIM).transpose(1, 0, 2)
    w2k = np.concatenate([w2k, w2k], 2)
    w2v = a(cmp_w2_v)[0].reshape(2, P, HEAD_DIM).transpose(1, 0, 2)
    xT = x.T.reshape(KT, P, SEQ).transpose(1, 0, 2).reshape(P, KT * SEQ)
    x_res = x.reshape(TT, P, D_MODEL)[::-1].transpose(1, 0, 2).reshape(P, TT * D_MODEL)
    gain_bias = np.concatenate([a(ln_gain)[0], a(ln_bias)[0]])

    nc = bacc.Bacc("TRN2", target_bir_lowering=False, num_devices=1)
    arrays, args = {}, []
    for name, v in (("xT", xT), ("w_full", w_full), ("w_nv", w_nv), ("w1", w1), ("kmat", constants()), ("pos", pos),
                    ("b1", b1), ("w2k", w2k), ("w2v", w2v), ("x_res", x_res), ("gain_bias", gain_bias)):
        v = np.ascontiguousarray(v)
        arrays[f"in_{name}"] = v
        args.append(nc.dram_tensor(f"in_{name}", v.shape, mybir.dt.from_np(v.dtype), kind="ExternalInput").ap())
    out = nc.dram_tensor("out_0", (SEQ, D_MODEL), mybir.dt.float32, kind="ExternalOutput").ap()
    build(nc, *args, out)
    r = run_bass_kernel_spmd(nc, [arrays], core_ids=[0])
    return r.results[0]["out_0"].reshape(1, SEQ, D_MODEL)
```

```python
import numpy as np
import concourse.bass as bass
from concourse import mybir
from contextlib import ExitStack

P = 128
SEQ, D_MODEL, HEAD_DIM = 256, 1024, 64
TT = SEQ // P
KT = D_MODEL // P
GROUPS, REPS = 2, 4
D_NSA, D_MOBA = 512, 512
KV = GROUPS * HEAD_DIM
CH = 512
GATES = 3 * GROUPS * REPS
NARROW = 2 * KV + GATES
ROPE, HALF = HEAD_DIM // 4, HEAD_DIM // 8
ROPE_THETA = 500000.0
CMP_BLOCK, CMP_STRIDE, CMP_HIDDEN = 32, 16, 256
NCMP = SEQ // CMP_STRIDE - 1
CPAD = 16
CKT = CMP_BLOCK * HEAD_DIM // P
LN_EPS = 1e-5
ALPHA = 2.0 ** 0.25
NEG = -1e30
SCALE = HEAD_DIM ** -0.5

C_KV, C_NQ, C_NV, C_MK, C_MQ, C_MV, C_NZ, C_MZ, C_OA, C_OB = range(10)
STEPS = 4 * 8
UNIT0 = 12
UNITS = 18
RAW, HL, PIECE = 5, 3, 4 * CH

PIECES = ([("x", 0, 0)] + [("w", c, k) for c in (C_KV, C_NQ) for k in (0, 1)]
          + [("w", c, k) for c in (C_NV, C_MK) for k in (0, 1)]
          + [("fk", 0, 0), ("fk", 0, 1), ("fv", 1, 0), ("fv", 1, 1)]
          + [("w", c, k) for c in (C_MQ, C_MV, C_NZ, C_MZ, C_OA, C_OB) for k in (0, 1)]
          + [("res", 0, 0), ("gb", 0, 0)])

WARM_UP = 10

FIRST = [(kt, 1) for kt in range(KT)]

OUT_PARTS = [(0, 0, CH), (0, CH, CH), (1, 0, CH), (1, CH, CH // 2), (1, CH + CH // 2, CH // 2)]
SHARE = 320

TURNS = [("kv0", "both"), ("kv1", "both"), ("qraw0", "act"), ("qraw1", "act"),
         ("qrot0", "both"), ("qrot1", "both"), ("hk", "dve"), ("hv", "dve"), ("hT", "both"),
         ("p0", "both"), ("kcvc", "dve"), ("p1", "both"), ("cs", "dve"), ("p2", "both"),
         ("p3", "both"), ("mk0", "both"), ("p4", "both"), ("p5", "both"), ("mk1", "both"), ("p6", "both"),
         ("mq0", "both"), ("p7", "both"), ("p8", "both"), ("mq1", "both"), ("p9", "both"),
         ("p10", "both"), ("cp", "act"), ("p11", "both"), ("p12", "both"), ("oc0", "dve"), ("p13", "both"), ("zn0", "act"),
         ("p14", "both"), ("oc1", "dve"), ("p15", "both"), ("zn1", "act"), ("p16", "both"),
         ("p17", "both"), ("zm0", "act"), ("zm1", "act")]
TURN_AT = {name: n for n, (name, _) in enumerate(TURNS)}


def act_turns(name):
    return sum(who != "dve" for _, who in TURNS[:TURN_AT[name] + 1])


def dve_turns(name):
    return sum(who != "act" for _, who in TURNS[:TURN_AT[name] + 1])


def unit_of(i):
    return i // 3, i % 3


def width(c):
    return NARROW if c == C_NV else CH


def sections_before(c):
    return 2 * (C_KV, C_NQ, C_MK, C_MQ).index(c)


def units_before(m):
    return 3 * m + 3 if m < 4 else 15 if m < 6 else 18


K_IDENT, K_SEL, K_CVALID, K_BLOCK, K_COS, K_SIN, K_CAUSAL, K_CMASK = range(8)
K_SIZES = [P, P, TT * CPAD, GROUPS * REPS, TT * ROPE, TT * ROPE, P, TT * P]
K_AT = [sum(K_SIZES[:n]) for n in range(len(K_SIZES) + 1)]
K_KEPT = K_AT[K_CAUSAL]


def constants():
    k = np.zeros((P, K_AT[-1]), np.float32)
    at = lambda n: k[:, K_AT[n]:K_AT[n + 1]]
    row = np.arange(P)
    at(K_IDENT)[:] = np.eye(P)
    at(K_SEL)[:] = ((row[:, None] % 32 // CPAD == row[None, :] // (REPS * CPAD))
                    & (row[:, None] % CPAD == row[None, :] % CPAD))
    at(K_CAUSAL)[:] = np.where(row[None, :] > row[:, None], NEG, 0.0)
    c = np.arange(CPAD)
    for t in range(TT):
        ok = (c[None, :] * CMP_STRIDE + CMP_BLOCK - 1 <= (t * P + row)[:, None]) & (c[None, :] < NCMP)
        at(K_CVALID)[:, t * CPAD:(t + 1) * CPAD] = ok
        at(K_CMASK)[:, t * P:(t + 1) * P] = np.tile(np.where(ok, 0.0, NEG), (1, P // CPAD))
    at(K_BLOCK)[:] = 0.5 * (row[:, None] // CPAD == np.arange(P // CPAD)[None, :])
    inv = np.float32(ROPE_THETA) ** (-np.arange(0, ROPE, 2, dtype=np.float32) / np.float32(ROPE))
    ang = np.arange(SEQ, dtype=np.float32)[:, None] * inv[None, :].astype(np.float32)
    cos, sin = np.cos(ang), np.sin(ang)
    for t in range(TT):
        rows = slice(t * P, (t + 1) * P)
        at(K_COS)[:, t * ROPE:(t + 1) * ROPE] = np.concatenate([cos[rows], cos[rows]], 1)
        at(K_SIN)[:, t * ROPE:(t + 1) * ROPE] = np.concatenate([-sin[rows], sin[rows]], 1)
    return k


def build(nc, xT, w_full, w_nv, w1, kmat, pos, b1, w2k, w2v, x_res, gain_bias, out):
    f32, f32r, bf16 = mybir.dt.float32, mybir.dt.float32r, mybir.dt.bfloat16
    ALU, ACT, AX = mybir.AluOpType, mybir.ActivationFunctionType, mybir.AxisListType
    ctx = ExitStack()
    with ctx:
        def sb(name, shape, dt=f32):
            return ctx.enter_context(nc.sbuf_tensor(name, shape, dt))

        def ps(name):
            return ctx.enter_context(nc.psum_tensor(name, [P, CH], f32))

        def sem(name):
            return ctx.enter_context(nc.semaphore(name))

        raw = sb("raw", [P, RAW, PIECE])
        w_hi = sb("w_hi", [P, HL, 4, CH], f32r)
        w_lo = sb("w_lo", [P, HL, 4, CH], f32r)
        x_hi = sb("x_hi", [P, KT, SEQ], f32r)
        x_lo = sb("x_lo", [P, KT, SEQ], f32r)
        k_sb = sb("k_sb", [P, K_KEPT])
        ident_bf = sb("ident_bf", [P, P], bf16)
        causal_bf = sb("causal_bf", [P, P], bf16)
        cmask_bf = sb("cmask_bf", [P, TT, P], bf16)
        pos_sb = sb("pos_sb", [P, 2, 2, CKT])
        ones_sb = sb("ones_sb", [1, P])
        w2k_sb = sb("w2k_sb", [P, 2, HEAD_DIM])
        w2v_sb = sb("w2v_sb", [P, 2, HEAD_DIM])
        keys_tok = sb("keys_tok", [P, TT, CH])
        q_tok = sb("q_tok", [P, TT, CH])
        swapped = sb("swapped", [P, 8, ROPE])
        qraw_T = sb("qraw_T", [P, 4, SEQ])
        q_st = sb("q_st", [P, 8, SEQ], f32r)
        qm_st = sb("qm_st", [P, 8, SEQ], f32r)
        k_hi = sb("k_hi", [P, GROUPS, 2, SEQ], f32r)
        k_lo = sb("k_lo", [P, GROUPS, 2, SEQ], f32r)
        km_hi = sb("km_hi", [P, 8, SEQ], f32r)
        km_lo = sb("km_lo", [P, 8, SEQ], f32r)
        kvc_T = sb("kvc_T", [P, 2, SEQ])
        cmp_in = sb("cmp_in", [P, 2, CKT, 2 * CPAD])
        hid_parts = sb("hid_parts", [P, 2, CMP_HIDDEN])
        hid = sb("hid", [P, 2, 2, P])
        b1_sb = hid[0:1, :, :, :].rearrange("p a b n -> p a (b n)")
        kc_B = sb("kc_B", [P, GROUPS, 2 * CPAD])
        vc_B = sb("vc_B", [P, 4, P])
        cmp_p = sb("cmp_p", [P, TT, P])
        cmp_stat = sb("cmp_stat", [P, 3, TT, 8])
        cmp_pT = sb("cmp_pT", [P, SEQ])
        v_st = sb("v_st", [P, TT, 2 * GROUPS, P], f32r)
        vm_st = sb("vm_st", [P, TT, 8, P], f32r)
        gates = sb("gates", [P, TT, GATES])
        probs = sb("probs", [P, 2, CH])
        pT_hi = sb("pT_hi", [P, 2, 4, P], f32r)
        pT_lo = sb("pT_lo", [P, 2, 4, P], f32r)
        masks = probs[:, 0, 0:3 * P]
        neg_max = sb("neg_max", [P, 2, 4])
        row_sum = sb("row_sum", [P, 2, 4])
        inverse = sb("inverse", [P, 4])
        weight = sb("weight", [P, 2, 4])
        o_T = sb("o_T", [P, 8, SEQ])
        stats = sb("stats", [P, TT, 4, 6])
        moments = sb("moments", [P, TT, 2])
        rstd = sb("rstd", [P, TT, 3])
        zT = [qraw_T[:, :, :],
              cmp_in[:, :, :, :].rearrange("p a b c -> p (a b c)").rearrange("p (m t) -> p m t", m=4)]
        y_parts = [q_st, qm_st]

        acc = [ps(f"acc{n}") for n in range(2)]
        scores = [ps(f"scores{n}") for n in range(2)]
        turn = [ps(f"turn{n}") for n in range(2)]
        heads = [ps(f"heads{n}") for n in range(2)]

        raw_in = [sem(f"raw_in{n}") for n in range(RAW)]
        x_in = [sem(f"x_in{n}") for n in range(len(FIRST))]
        w_in = [sem(f"w_in{n}") for n in range(len(FIRST))]
        nq_in = [sem(f"nq_in{n}") for n in range(4)]
        first_hi, first_lo = sem("first_hi"), sem("first_lo")
        k_in, mask_in, pos_in, b1_in, w2k_in, w2v_in = (sem(n) for n in ("k_in", "mask_in", "pos_in", "b1_in", "w2k_in", "w2v_in"))
        x_hi_ok, x_lo_ok = sem("x_hi_ok"), sem("x_lo_ok")
        hi_ok, lo_ok = sem("hi_ok"), sem("lo_ok")
        bf_ok = sem("bf_ok")
        idle_ok = sem("idle_ok")
        zero_ok = sem("zero_ok")
        group_done = sem("group_done")
        acc_read = sem("acc_read")
        z_tanh, z_read = sem("z_tanh"), sem("z_read")
        gates_tanh, gates_ok = sem("gates_tanh"), sem("gates_ok")
        rope_a, rope_ok = sem("rope_a"), sem("rope_ok")
        turn_full = sem("turn_full")
        turn_act, turn_dve = sem("turn_act"), sem("turn_dve")
        km_in = [sem(f"km_in{n}") for n in range(2)]
        packed = sem("packed")
        hid_read = sem("hid_read")
        scores_ok, max_ok, probs_ok = sem("scores_ok"), sem("max_ok"), sem("probs_ok")
        weight_ok, scaled_ok = sem("weight_ok"), sem("scaled_ok")
        heads_ok, heads_hi, heads_read = sem("heads_ok"), sem("heads_hi"), sem("heads_read")
        v_hi_ok, v_ok = sem("v_hi_ok"), sem("v_ok")
        link_done = sem("link_done")
        cmp_shift, cmp_exp, cmp_pok = sem("cmp_shift"), sem("cmp_exp"), sem("cmp_pok")
        oT_ok, y_ok, y_hi_ok, y_lo_ok = sem("oT_ok"), sem("y_ok"), sem("y_hi_ok"), sem("y_lo_ok")
        out_ok = sem("out_ok")
        mom_ok, eps_ok, rstd_ok = sem("mom_ok"), sem("eps_ok"), sem("rstd_ok")
        centred, spread = sem("centred"), sem("spread")
        fin_pool, fin_dve = sem("fin_pool"), sem("fin_dve")
        stored = [sem(f"stored{n}") for n in range(5)]

        const = lambda n: k_sb[:, K_AT[n]:K_AT[n + 1]]
        ident = const(K_IDENT)
        out_bank = [acc[0], scores[0], acc[1], scores[1], turn[TURN_AT["zm0"] % 2]]
        stretches = [(0, slice(0, CH)), (0, slice(CH, D_MODEL)), (1, slice(0, SHARE)),
                     (1, slice(SHARE, (SHARE + D_MODEL) // 2)), (1, slice((SHARE + D_MODEL) // 2, D_MODEL))]
        res = PIECES.index(("res", 0, 0))
        gb = PIECES.index(("gb", 0, 0))
        x_tok = raw[:, res % RAW, :].rearrange("p (t n) -> p t n", t=TT)
        total = raw[:, (gb - 3) % RAW, :].rearrange("p (t n) -> p t n", t=TT)
        gain = raw[:, gb % RAW, 0:D_MODEL]
        bias = raw[:, gb % RAW, D_MODEL:2 * D_MODEL]

        def wait_piece(eng, piece):
            n = PIECES.index(piece)
            eng.wait_ge(raw_in[n % RAW], 16 * (n // RAW))

        def wait_turn_free(eng, name):
            n = TURN_AT[name]
            if n >= 2:
                old, who = TURNS[n - 2]
                if who == "act":
                    eng.wait_ge(turn_act, act_turns(old))
                else:
                    eng.wait_ge(turn_dve, dve_turns(old))

        def wait_turn(eng, name):
            eng.wait_ge(turn_full, TURN_AT[name] + 1)

        def turn_bank(name):
            return turn[TURN_AT[name] % 2]

        block = ctx.enter_context(nc.Block())

        @block.sync
        def _(sp):
            for n, (kt, count) in enumerate(FIRST):
                part = slice(kt * SEQ, (kt + count) * SEQ)
                sp.dma_start(raw[:, 0, part], xT[:, part]).then_inc(x_in[n], 16)
                part = slice(kt % 4 * CH, (kt % 4 + count) * CH)
                sp.dma_start(raw[:, 1 + kt // 4, part], w_full[kt // 4][:, part]).then_inc(w_in[n], 16)
            for u in range(4):
                part = slice(u % 2 * 2 * CH, (u % 2 + 1) * 2 * CH)
                sp.dma_start(raw[:, 3 + u // 2, part], w_full[2 * C_NQ + u // 2][:, part]).then_inc(nq_in[u], 16)
                if u == 1:
                    sp.dma_start(k_sb[:, :], kmat[:, 0:K_KEPT]).then_inc(k_in, 16)
            sp.dma_start(pos_sb[:, :, :, :], pos).then_inc(pos_in, 16)
            sp.dma_start(masks, kmat[:, K_KEPT:]).then_inc(mask_in, 16)
            sp.dma_start(b1_sb, b1).then_inc(b1_in, 16)
            sp.dma_start(w2k_sb[:, :, :], w2k).then_inc(w2k_in, 16)
            sp.dma_start(w2v_sb[:, :, :], w2v).then_inc(w2v_in, 16)
            for n, (kind, c, k) in enumerate(PIECES):
                if n < RAW:
                    continue
                old, oc, ok = PIECES[n - RAW]
                if old == "x":
                    sp.wait_ge(x_lo_ok, len(FIRST))
                elif old == "w":
                    sp.wait_ge(lo_ok, 4 * oc + 2 * ok + 2)
                elif ok == 0:
                    sp.wait_ge(hid_read, oc + 1)
                else:
                    wait_turn(sp, ("hk", "hv")[oc])
                dst = raw[:, n % RAW, :]
                if kind == "x":
                    src = xT
                elif kind == "w" and c == C_NV:
                    dst, src = raw[:, n % RAW, 0:4 * NARROW], w_nv[k]
                elif kind == "w":
                    src = w_full[2 * (c - (c > C_NV)) + k]
                elif kind == "res":
                    src = x_res
                elif kind == "gb":
                    src = gain_bias.partition_broadcast(P)
                else:
                    src = w1[c, k]
                sp.dma_start(dst, src).then_inc(raw_in[n % RAW], 16)
            for n in (0, 1, 3, 2, 4):
                t, cols = stretches[n]
                if n < 3:
                    sp.wait_ge(fin_pool, n + 1)
                else:
                    sp.wait_ge(fin_dve, n - 2)
                sp.dma_start(out[t * P:(t + 1) * P, cols], total[:, t, cols]).then_inc(stored[n], 16)
            for s in stored:
                sp.wait_ge(s, 16)

        @block.gpsimd
        def _(pool):
            pool.memset(hid_parts[:, 0, 0:P], 0.0).then_inc(idle_ok, 1)
            pool.memset(cmp_in[:, :, :, :], 0.0).then_inc(zero_ok, 1)
            pool.memset(kc_B[:, :, :], 0.0).then_inc(zero_ok, 1)
            pool.memset(ones_sb[:, :], 1.0).then_inc(zero_ok, 1)
            pool.memset(rstd[:, :, 2:3], -0.5).then_inc(eps_ok, 1)
            pool.wait_ge(k_in, 16)

            def rope(n):
                c, t = (C_KV, C_NQ, C_MK, C_MQ)[n // 2], n % 2
                pool.wait_ge(acc_read, sections_before(c) + t + 1)
                if c == C_NQ:
                    wait_turn(pool, f"qraw{t}")
                tok = keys_tok if c in (C_KV, C_MK) else q_tok
                at = 2 * KV if c == C_KV else 0
                nh = (CH - at) // HEAD_DIM
                v = tok[:, t, at:CH].rearrange("p (h d) -> p h d", d=HEAD_DIM)
                cos = const(K_COS)[:, t * ROPE:(t + 1) * ROPE].unsqueeze(1).broadcast_to((P, nh, ROPE))
                sin = const(K_SIN)[:, t * ROPE:(t + 1) * ROPE].unsqueeze(1).broadcast_to((P, nh, ROPE))
                part = swapped[:, 0:nh, :]
                if n:
                    pool.wait_ge(rope_ok, n)
                pool.tensor_tensor(part[:, :, 0:HALF], v[:, :, HALF:ROPE], sin[:, :, 0:HALF], ALU.mult).then_inc(rope_a, 1)
                pool.tensor_tensor(part[:, :, HALF:ROPE], v[:, :, 0:HALF], sin[:, :, HALF:ROPE], ALU.mult).then_inc(rope_a, 1)
                pool.wait_ge(rope_a, 3 * n + 2)
                pool.tensor_tensor(v[:, :, 0:ROPE], v[:, :, 0:ROPE], cos, ALU.mult).then_inc(rope_a, 1)
                pool.wait_ge(rope_a, 3 * n + 3)
                pool.tensor_tensor(v[:, :, 0:ROPE], v[:, :, 0:ROPE], part, ALU.add).then_inc(rope_ok, 1)

            def scale_probs(i):
                pool.wait_ge(weight_ok, i + 1)
                n = 2 if unit_of(i)[1] < 2 else 4
                v = probs[:, i % 2, :].rearrange("p (n k) -> p n k", n=n)
                pool.tensor_tensor(v, v, weight[:, i % 2, 0:n].unsqueeze(2).broadcast_to((P, n, CH // n)),
                                   ALU.mult).then_inc(scaled_ok, 1)

            for n in range(4):
                rope(n)
            for i in range(UNITS):
                if i in (2, 4, 6, 8):
                    rope(4 + (i - 2) // 2)
                scale_probs(i)
            for t in range(TT):
                pool.wait_ge(mom_ok, t + 1)
                pool.tensor_scalar(rstd[:, t, 0:1], moments[:, t, 1:2], LN_EPS, None, ALU.add).then_inc(eps_ok, 1)
                pool.wait_ge(eps_ok, t + 2)
                pool.tensor_tensor(rstd[:, t, 1:2], rstd[:, t, 0:1], rstd[:, t, 2:3], ALU.pow).then_inc(rstd_ok, 1)
                for n in ((0, 1), (2,))[t]:
                    pool.wait_ge(spread, n + 1)
                    if n == 0:
                        wait_piece(pool, ("gb", 0, 0))
                    cols = stretches[n][1]
                    pool.tensor_tensor(total[:, t, cols], total[:, t, cols], bias[:, cols], ALU.add).then_inc(fin_pool, 1)

        @block.scalar
        def _(act):
            def split_first(n):
                kt, count = FIRST[n]
                act.wait_ge(x_in[n], 16)
                act.activation(x_hi[:, kt:kt + count, :].rearrange("p k t -> p (k t)"),
                               raw[:, 0, kt * SEQ:(kt + count) * SEQ], ACT.Copy).then_inc(x_hi_ok, 1)
                act.wait_ge(w_in[n], 16)
                act.activation(w_hi[:, kt // 4, kt % 4:kt % 4 + count, :].rearrange("p k n -> p (k n)"),
                               raw[:, 1 + kt // 4, kt % 4 * CH:(kt % 4 + count) * CH],
                               ACT.Copy).then_inc(*((first_hi, 1) if n < len(FIRST) - 1 else (hi_ok, 4)))

            def split(u):
                c, k, j = u // 4, u % 4 // 2, u % 2
                piece = 2 * c + k
                if c == C_NQ:
                    act.wait_ge(nq_in[u % 4], 16)
                else:
                    wait_piece(act, ("w", c, k))
                if piece >= HL:
                    act.wait_ge(group_done, last_use(piece - HL))
                w = width(c)
                n = PIECES.index(("w", c, k))
                src = raw[:, n % RAW, 2 * j * w:2 * (j + 1) * w].rearrange("p (k n) -> p k n", k=2)
                act.activation(w_hi[:, piece % HL, 2 * j:2 * j + 2, 0:w], src, ACT.Copy).then_inc(hi_ok, 1)

            def copy_group(c, t):
                act.wait_ge(group_done, t + 3 if c == C_KV else 4 * c + 2 * t + 2)
                src = acc[t]
                if c == C_KV:
                    act.activation(keys_tok[:, t, :], src[:, :], ACT.Copy).then_inc(acc_read, 1)
                elif c == C_MK:
                    wait_turn(act, "kv1")
                    act.activation(keys_tok[:, t, :], src[:, :], ACT.Copy).then_inc(acc_read, 1)
                elif c == C_NQ:
                    act.activation(q_tok[:, t, :], src[:, :], ACT.Copy, scale=SCALE).then_inc(acc_read, 1)
                elif c == C_MQ:
                    wait_turn(act, "qrot1")
                    act.activation(q_tok[:, t, :], src[:, :], ACT.Copy, scale=SCALE).then_inc(acc_read, 1)
                elif c == C_NV:
                    act.activation(gates[:, t, :], src[:, 2 * KV:NARROW], ACT.Tanh, scale=0.5)
                    act.activation(v_st[:, t, :, 0:HEAD_DIM], src[:, 0:2 * KV].rearrange("p (n d) -> p n d", d=HEAD_DIM),
                                   ACT.Copy).then_inc(v_hi_ok, 1)
                elif c == C_MV:
                    act.activation(vm_st[:, t, :, 0:HEAD_DIM], src[:, :].rearrange("p (n d) -> p n d", d=HEAD_DIM),
                                   ACT.Copy).then_inc(v_hi_ok, 1)
                else:
                    wait_turn(act, "mk1" if c == C_NZ else "mq1")
                    z = keys_tok if c == C_NZ else q_tok
                    act.activation(z[:, t, :], src[:, :], ACT.Tanh, scale=0.5).then_inc(z_tanh, 1)

            def exps(i):
                n = 2 if unit_of(i)[1] < 2 else 4
                w = CH // n
                act.wait_ge(max_ok, i + 1)
                if i >= 2:
                    wait_turn(act, f"p{i - 2}")
                    act.wait_ge(weight_ok, i - 1)
                for h in range(n):
                    last = act.activation(probs[:, i % 2, h * w:(h + 1) * w], scores[i % 2][:, h * w:(h + 1) * w], ACT.Exp,
                                          bias=neg_max[:, i % 2, h:h + 1], accum_out=row_sum[:, i % 2, h:h + 1])
                last.then_inc(probs_ok, 1)

            def probs_hi(i):
                wait_turn(act, f"p{i}")
                if i >= 2:
                    act.wait_ge(heads_ok, i - 1)
                act.activation(pT_hi[:, i % 2, :, :].rearrange("p n q -> p (n q)"), turn_bank(f"p{i}")[:, :],
                               ACT.Copy).then_inc(turn_act, 1)

            def pairs_bank(name):
                return turn_bank(name)[:, :].rearrange("p (m t) -> p m t", m=4)

            def queries_hi(name, dst, t):
                wait_turn(act, name)
                pair = dst[0:64, :, t * P:(t + 1) * P].rearrange("p (m h) t -> p m h t", h=2)
                act.activation(pair[:, :, 0, :], pairs_bank(name)[0:64, :, :], ACT.Copy)
                act.activation(pair[:, :, 1, :], pairs_bank(name)[64:P, :, :], ACT.Copy).then_inc(turn_act, 1)

            def keys_hi(name, dst_of, n0, copies):
                wait_turn(act, name)
                for side in range(2):
                    for half in range(copies):
                        last = act.activation(dst_of(side)[64 * half:64 * half + 64],
                                              pairs_bank(name)[64 * side:64 * side + 64, n0:4, :], ACT.Copy)
                last.then_inc(turn_act, 1)

            def nsa_keys(t):
                if t == 0:
                    wait_turn(act, "kv0")
                else:
                    wait_turn(act, "kv1")
                act.activation(kvc_T[:, :, t * P:(t + 1) * P], pairs_bank(f"kv{t}")[:, 0:2, :], ACT.Copy)
                keys_hi(f"kv{t}", lambda side: k_hi[:, side, :, t * P:(t + 1) * P], 2, 2)

            def moba_keys(t):
                keys_hi(f"mk{t}", lambda side: km_hi[:, side::2, t * P:(t + 1) * P], 0, 1)

            def heads_start(m):
                act.wait_ge(heads_ok, units_before(m))
                for h in range(2):
                    last = act.activation(o_T[64 * h:64 * h + 64, m, :], heads[m % 2][0:64, h * SEQ:(h + 1) * SEQ], ACT.Copy)
                last.then_inc(heads_hi, 1)

            def gate_out(name, half, t):
                wait_turn(act, name)
                wait_turn(act, ("cs", "hv")[half])
                act.activation(zT[half][:, :, t * P:(t + 1) * P], pairs_bank(name), ACT.Copy, scale=0.5).then_inc(turn_act, 1)

            def y_hi(half, t):
                act.wait_ge(y_ok, 2 * half + t + 1)
                act.wait_ge(scores_ok, 12 if half == 0 else UNITS)
                tok = slice(t * P, (t + 1) * P)
                act.activation(y_parts[half][:, 0:4, tok], o_T[:, 4 * half:4 * half + 4, tok], ACT.Copy).then_inc(y_hi_ok, 1)

            for n in range(len(FIRST)):
                split_first(n)
            for s in range(STEPS):
                i = s - UNIT0
                if 0 <= i - 3 < UNITS:
                    probs_hi(i - 3)
                if s == 20:
                    moba_keys(1)
                if 0 <= i - 1 < UNITS:
                    exps(i - 1)
                if s == 3:
                    copy_group(C_KV, 0)
                if s == 4:
                    copy_group(C_KV, 1)
                elif s % 2 == 0 and s > 4:
                    copy_group((s - 1) // 4, (s - 1) % 4 // 2)
                if s == 5:
                    nsa_keys(0)
                if s == 6:
                    nsa_keys(1)
                if s == 7:
                    wait_turn(act, "qraw0")
                    act.activation(qraw_T[:, :, 0:P], pairs_bank("qraw0"), ACT.Copy).then_inc(turn_act, 1)
                if s == 9:
                    wait_turn(act, "qraw1")
                    act.activation(qraw_T[:, :, P:SEQ], pairs_bank("qraw1"), ACT.Copy).then_inc(turn_act, 1)
                if s == 10:
                    queries_hi("qrot0", q_st, 0)
                if s == 12:
                    queries_hi("qrot1", q_st, 1)
                if s == 14:
                    wait_turn(act, "hT")
                    act.activation(hid[:, :, :, :], turn_bank("hT")[:, :].rearrange("p (a b n) -> p a b n", a=2, b=2),
                                   ACT.Tanh, scale=0.5).then_inc(turn_act, 1)
                if s == 16:
                    act.wait_ge(cmp_shift, 1)
                    act.activation(cmp_p[:, :, :], cmp_p[:, :, :], ACT.Exp).then_inc(cmp_exp, 1)
                if s == 18:
                    moba_keys(0)
                if s == 25:
                    wait_turn(act, "cp")
                    act.activation(cmp_pT[:, :], turn_bank("cp")[:, 0:SEQ], ACT.Copy).then_inc(turn_act, 1)
                if s in (19, 22, 25, 27):
                    heads_start((s - 18) // 3)
                if s == 21:
                    act.wait_ge(turn_dve, dve_turns("mk1"))
                    act.dma_start(km_hi[64:P, :, :].bitcast(f32), km_hi[0:64, :, :].bitcast(f32)).then_inc(km_in[0], 16)
                    act.dma_start(km_lo[64:P, :, :].bitcast(f32), km_lo[0:64, :, :].bitcast(f32)).then_inc(km_in[1], 16)
                if s == 21:
                    queries_hi("mq0", qm_st, 0)
                if s == 23:
                    queries_hi("mq1", qm_st, 1)
                if s == 28:
                    gate_out("zn0", 0, 0)
                if s == 30:
                    heads_start(4)
                    heads_start(5)
                    gate_out("zn1", 0, 1)
                    y_hi(0, 0)
                if s == 31:
                    y_hi(0, 1)
                for u in splits_in(s):
                    split(u)
            probs_hi(17)
            copy_group(C_MZ, 1)
            gate_out("zm0", 1, 0)
            split(4 * C_OB)
            split(4 * C_OB + 1)
            heads_start(6)
            heads_start(7)
            gate_out("zm1", 1, 1)
            y_hi(1, 0)
            y_hi(1, 1)
            split(4 * C_OB + 2)
            split(4 * C_OB + 3)
            for n, (t, cols) in enumerate(stretches[:3]):
                act.wait_ge(centred, n + 1)
                act.wait_ge(rstd_ok, t + 1)
                act.activation(total[:, t, cols], total[:, t, cols], ACT.Copy, scale=rstd[:, t, 1:2]).then_inc(spread, 1)

        @block.vector
        def _(dve):
            chain = [0]

            def link(instruction):
                chain[0] += 1
                instruction.then_inc(link_done, 1)
                dve.wait_ge(link_done, chain[0])

            def split_first(n):
                kt, count = FIRST[n]
                dve.wait_ge(x_hi_ok, n + 1)
                dve.tensor_tensor(x_lo[:, kt:kt + count, :].rearrange("p k t -> p (k t)"),
                                  raw[:, 0, kt * SEQ:(kt + count) * SEQ],
                                  x_hi[:, kt:kt + count, :].bitcast(f32).rearrange("p k t -> p (k t)"),
                                  ALU.subtract).then_inc(x_lo_ok, 1)
                if n < len(FIRST) - 1:
                    dve.wait_ge(first_hi, n + 1)
                else:
                    dve.wait_ge(hi_ok, 4)
                dve.tensor_tensor(w_lo[:, kt // 4, kt % 4:kt % 4 + count, :].rearrange("p k n -> p (k n)"),
                                  raw[:, 1 + kt // 4, kt % 4 * CH:(kt % 4 + count) * CH],
                                  w_hi[:, kt // 4, kt % 4:kt % 4 + count, :].bitcast(f32).rearrange("p k n -> p (k n)"),
                                  ALU.subtract).then_inc(*((first_lo, 1) if n < len(FIRST) - 1 else (lo_ok, 4)))

            def split(u):
                c, k, j = u // 4, u % 4 // 2, u % 2
                piece = 2 * c + k
                w = width(c)
                n = PIECES.index(("w", c, k))
                dve.wait_ge(hi_ok, u + 1)
                src = raw[:, n % RAW, 2 * j * w:2 * (j + 1) * w].rearrange("p (k n) -> p k n", k=2)
                at = (slice(None), piece % HL, slice(2 * j, 2 * j + 2), slice(0, w))
                dve.tensor_tensor(w_lo[at], src, w_hi[at].bitcast(f32), ALU.subtract).then_inc(lo_ok, 1)

            def values_lo(c, t):
                dve.wait_ge(v_hi_ok, 2 * (c == C_MV) + t + 1)
                st = v_st if c == C_NV else vm_st
                n = 2 * GROUPS if c == C_NV else 8
                dve.tensor_tensor(st[:, t, :, HEAD_DIM:P], acc[t][:, 0:n * HEAD_DIM].rearrange("p (n d) -> p n d", d=HEAD_DIM),
                                  st[:, t, :, 0:HEAD_DIM].bitcast(f32), ALU.subtract).then_inc(v_ok, 1)

            def silu_out(c, t):
                dve.wait_ge(z_tanh, 2 * (c - C_NZ) + t + 1)
                part = (keys_tok if c == C_NZ else q_tok)[:, t, :]
                dve.scalar_tensor_tensor(part, part, 1.0, acc[t][:, :], ALU.add, ALU.mult).then_inc(z_read, 1)

            def maxima(i):
                dve.wait_ge(scores_ok, i + 1)
                if i >= 2:
                    dve.wait_ge(probs_ok, i - 1)
                n = 2 if unit_of(i)[1] < 2 else 4
                dve.tensor_reduce(neg_max[:, i % 2, 0:n], scores[i % 2][:, :].rearrange("p (n k) -> p n k", n=n),
                                  AX.X, ALU.max, negate=True).then_inc(max_ok, 1)

            def probs_lo(i):
                dve.wait_ge(turn_act, act_turns(f"p{i}"))
                dve.tensor_tensor(pT_lo[:, i % 2, :, :].rearrange("p n q -> p (n q)"), turn_bank(f"p{i}")[:, :],
                                  pT_hi[:, i % 2, :, :].bitcast(f32).rearrange("p n q -> p (n q)"),
                                  ALU.subtract).then_inc(turn_dve, 1)

            def weights(i):
                g, kind = unit_of(i)
                n = 2 if kind < 2 else 4
                dve.wait_ge(probs_ok, i + 1)
                if i >= 2:
                    dve.wait_ge(scaled_ok, i - 1)
                if g >= 4:
                    dve.reciprocal(weight[:, i % 2, 0:n], row_sum[:, i % 2, 0:n]).then_inc(weight_ok, 1)
                    return
                link(dve.reciprocal(inverse[:, 0:n], row_sum[:, i % 2, 0:n]))
                if kind < 2:
                    gate = gates[:, 1, (1 + kind) * 8 + 2 * g:(1 + kind) * 8 + 2 * g + 2]
                    dve.tensor_tensor(weight[:, i % 2, 0:2], inverse[:, 0:2], gate, ALU.mult).then_inc(weight_ok, 1)
                else:
                    gate = gates[:, 0, 8:24].rearrange("p (b h) -> p h b", b=2)[:, 2 * g:2 * g + 2, :]
                    dve.tensor_tensor(weight[:, i % 2, :].rearrange("p (h b) -> p h b", h=2),
                                      inverse[:, :].rearrange("p (h b) -> p h b", h=2), gate, ALU.mult).then_inc(weight_ok, 1)

            def pairs_bank(name):
                return turn_bank(name)[:, :].rearrange("p (m t) -> p m t", m=4)

            def queries_lo(name, dst, t):
                dve.wait_ge(turn_act, act_turns(name))
                tok = slice(t * P, (t + 1) * P)
                hi = dst[0:64, :, tok].bitcast(f32).rearrange("p (m h) t -> p m h t", h=2)
                lo = dst[64:P, :, tok].rearrange("p (m h) t -> p m h t", h=2)
                dve.tensor_tensor(lo[:, :, 0, :], pairs_bank(name)[0:64, :, :], hi[:, :, 0, :], ALU.subtract)
                dve.tensor_tensor(lo[:, :, 1, :], pairs_bank(name)[64:P, :, :], hi[:, :, 1, :], ALU.subtract).then_inc(turn_dve, 1)

            def keys_lo(name, hi_of, lo_of, n0, copies):
                dve.wait_ge(turn_act, act_turns(name))
                for side in range(2):
                    for half in range(copies):
                        rows = slice(64 * half, 64 * half + 64)
                        last = dve.tensor_tensor(lo_of(side)[rows], pairs_bank(name)[64 * side:64 * side + 64, n0:4, :],
                                                 hi_of(side)[rows].bitcast(f32), ALU.subtract)
                last.then_inc(turn_dve, 1)

            def nsa_keys_lo(t):
                tok = slice(t * P, (t + 1) * P)
                keys_lo(f"kv{t}", lambda side: k_hi[:, side, :, tok], lambda side: k_lo[:, side, :, tok], 2, 2)

            def moba_keys_lo(t):
                tok = slice(t * P, (t + 1) * P)
                keys_lo(f"mk{t}", lambda side: km_hi[:, side::2, tok], lambda side: km_lo[:, side::2, tok], 0, 1)

            def heads_add(m):
                dve.wait_ge(heads_hi, m + 1)
                for h in range(2):
                    rows = slice(64 * h, 64 * h + 64)
                    last = dve.tensor_tensor(o_T[rows, m, :], heads[m % 2][64:P, h * SEQ:(h + 1) * SEQ], o_T[rows, m, :], ALU.add)
                last.then_inc(heads_read, 1)

            def compressed_add(half):
                wait_turn(dve, f"oc{half}")
                dve.wait_ge(heads_read, 2 * half + 2)
                part = o_T[:, 2 * half:2 * half + 2, :].rearrange("p m t -> p (m t)")
                dve.tensor_tensor(part, turn_bank(f"oc{half}")[:, :], part, ALU.add).then_inc(turn_dve, 1)

            def gate_y(half, t):
                if half == 0:
                    dve.wait_ge(turn_dve, dve_turns("oc1"))
                else:
                    dve.wait_ge(heads_read, 8)
                dve.wait_ge(turn_act, act_turns(("zn", "zm")[half] + str(t)))
                tok = slice(t * P, (t + 1) * P)
                part = o_T[:, 4 * half:4 * half + 4, tok]
                dve.tensor_tensor(part, part, zT[half][:, :, tok], ALU.mult).then_inc(y_ok, 1)

            def y_lo(half, t):
                dve.wait_ge(y_hi_ok, 2 * half + t + 1)
                tok = slice(t * P, (t + 1) * P)
                dve.tensor_tensor(y_parts[half][:, 4:8, tok], o_T[:, 4 * half:4 * half + 4, tok],
                                  y_parts[half][:, 0:4, tok].bitcast(f32), ALU.subtract).then_inc(y_lo_ok, 1)

            def pack(kind):
                for g in range(GROUPS):
                    rows = slice(64 * g, 64 * g + 64)
                    src = kvc_T[rows, kind, :].rearrange("p (c w) -> p c w", w=CMP_STRIDE)
                    for parity in range(2):
                        for half in range(2):
                            n = CKT // 2
                            v = src[:, half:half + NCMP, parity::2].rearrange("p c k -> p k c")
                            term = pos_sb[rows, kind, parity, half * n:(half + 1) * n].unsqueeze(2).broadcast_to((64, n, NCMP))
                            dve.tensor_tensor(cmp_in[64 * parity:64 * parity + 64, kind, half * n:(half + 1) * n,
                                                     g * CPAD:g * CPAD + NCMP], v, term, ALU.add).then_inc(packed, 1)

            for n in range(len(FIRST)):
                split_first(n)
            for s in range(STEPS):
                i = s - UNIT0
                if 0 <= i - 1 < UNITS:
                    maxima(i - 1)
                if 0 <= i - 3 < UNITS:
                    probs_lo(i - 3)
                if s == 20:
                    moba_keys_lo(1)
                for u in low_splits_in(s):
                    split(u)
                if 0 <= i - 1 < UNITS:
                    weights(i - 1)
                if s % 2 == 0 and (s - 1) // 4 in (C_NV, C_MV):
                    values_lo((s - 1) // 4, (s - 1) % 4 // 2)
                if s % 2 == 0 and (s - 1) // 4 >= C_NZ:
                    silu_out((s - 1) // 4, (s - 1) % 4 // 2)
                if s == 5:
                    nsa_keys_lo(0)
                if s == 6:
                    nsa_keys_lo(1)
                    dve.wait_ge(pos_in, 16)
                    dve.wait_ge(zero_ok, 1)
                    pack(0)
                if s == 7:
                    dve.wait_ge(k_in, 16)
                    dve.wait_ge(mask_in, 16)
                    dve.tensor_copy(ident_bf[:, :], ident)
                    dve.tensor_copy(causal_bf[:, :], masks[:, 0:P])
                    dve.tensor_copy(cmask_bf[:, :, :], masks[:, P:3 * P].rearrange("p (t n) -> p t n", t=TT)).then_inc(bf_ok, 1)
                if s == 8:
                    pack(1)
                if s == 10:
                    queries_lo("qrot0", q_st, 0)
                if s == 12:
                    queries_lo("qrot1", q_st, 1)
                    wait_turn(dve, "hk")
                    dve.tensor_copy(hid_parts[:, 0, :], turn_bank("hk")[:, 0:CMP_HIDDEN]).then_inc(turn_dve, 1)
                    link(dve.tensor_scalar(gates[:, :, :], gates[:, :, :], 1.0, 0.5, ALU.add, ALU.mult))
                if s == 13:
                    wait_turn(dve, "hv")
                    dve.tensor_copy(hid_parts[:, 1, :], turn_bank("hv")[:, 0:CMP_HIDDEN]).then_inc(turn_dve, 1)
                if s == 14:
                    dve.wait_ge(turn_act, act_turns("hT"))
                    dve.scalar_tensor_tensor(hid[:, :, :, :].rearrange("p a b n -> p (a b n)"),
                                             hid[:, :, :, :].rearrange("p a b n -> p (a b n)"), 1.0,
                                             turn_bank("hT")[:, :], ALU.add, ALU.mult).then_inc(turn_dve, 1)
                if s == 15:
                    wait_turn(dve, "kcvc")
                    b = turn_bank("kcvc")
                    keys = b[:, 0:GROUPS * CPAD].rearrange("p (g c) -> p g c", g=GROUPS)
                    dve.wait_ge(zero_ok, 2)
                    dve.tensor_scalar(kc_B[0:64, :, 0:CPAD], keys[0:64], 0.5, None, ALU.mult)
                    dve.tensor_scalar(kc_B[64:P, :, CPAD:2 * CPAD], keys[64:P], 0.5, None, ALU.mult)
                    dve.tensor_tensor(vc_B[:, :, :].rearrange("p m (h d) -> p (m h) d", d=HEAD_DIM),
                                      b[:, 64:P].unsqueeze(1).broadcast_to((P, 8, HEAD_DIM)),
                                      const(K_BLOCK).unsqueeze(2).broadcast_to((P, 8, HEAD_DIM)), ALU.mult).then_inc(turn_dve, 1)
                if s == 16:
                    wait_turn(dve, "cs")
                    b = turn_bank("cs")[:, 0:TT * P].rearrange("p (n c) -> p n c", c=CPAD)
                    stat = lambda n: cmp_stat[:, n, :, :].rearrange("p t h -> p (t h)")
                    wide = lambda n: stat(n).unsqueeze(2).broadcast_to((P, TT * 8, CPAD))
                    e = cmp_p[:, :, :].rearrange("p t (h c) -> p (t h) c", c=CPAD)
                    link(dve.tensor_reduce(stat(0), b, AX.X, ALU.max, negate=True))
                    dve.tensor_tensor(e, b, wide(0), ALU.add).then_inc(turn_dve, 1)
                    dve.wait_ge(turn_dve, dve_turns("cs"))
                    dve.memset(inverse[:, 0:1], 0.0).then_inc(cmp_shift, 1)
                if s == 17:
                    dve.wait_ge(cmp_exp, 1)
                    for t2 in range(TT):
                        e2 = cmp_p[:, t2, :].rearrange("p (h c) -> p h c", c=CPAD)
                        last = dve.tensor_tensor(e2, e2, const(K_CVALID)[:, t2 * CPAD:(t2 + 1) * CPAD].unsqueeze(1)
                                                 .broadcast_to((P, 8, CPAD)), ALU.mult)
                    link(last)
                    link(dve.tensor_reduce(stat(1), e, AX.X, ALU.add))
                    link(dve.tensor_scalar(stat(1), stat(1), 0.5, None, ALU.max))
                    link(dve.reciprocal(stat(2), stat(1)))
                    link(dve.tensor_tensor(cmp_stat[:, 2, :, :], cmp_stat[:, 2, :, :], gates[:, :, 0:8], ALU.mult))
                    dve.tensor_tensor(e, e, wide(2), ALU.mult).then_inc(cmp_pok, 1)
                if s in (19, 22, 25, 27):
                    heads_add((s - 18) // 3)
                if s == 18:
                    moba_keys_lo(0)
                if s == 21:
                    queries_lo("mq0", qm_st, 0)
                if s == 23:
                    queries_lo("mq1", qm_st, 1)
                if s == 27:
                    compressed_add(0)
                if s == 29:
                    compressed_add(1)
                    gate_y(0, 0)
                if s == 30:
                    heads_add(4)
                    heads_add(5)
                    gate_y(0, 1)
                    y_lo(0, 0)
                if s == 31:
                    y_lo(0, 1)
                if s % 4 == 3:
                    split(s + 3)
            probs_lo(17)
            silu_out(C_MZ, 1)
            split(4 * C_OB - 1)
            split(4 * C_OB)
            split(4 * C_OB + 1)
            heads_add(6)
            heads_add(7)
            gate_y(1, 0)
            gate_y(1, 1)
            y_lo(1, 0)
            y_lo(1, 1)
            split(4 * C_OB + 2)
            split(4 * C_OB + 3)
            wait_piece(dve, ("res", 0, 0))
            wait_piece(dve, ("gb", 0, 0))

            def centre(n):
                t, cols = stretches[n]
                return dve.scalar_tensor_tensor(total[:, t, cols], total[:, t, cols], moments[:, t, 0:1], gain[:, cols],
                                                ALU.subtract, ALU.mult)

            for t in range(TT):
                size = (CH, CH // 2)[t]
                for n, (tile, col, w) in enumerate(OUT_PARTS):
                    if tile == t:
                        dve.wait_ge(out_ok, n + 1)
                        link(dve.scalar_tensor_tensor(total[:, t, col:col + w], x_tok[:, t, col:col + w], ALPHA,
                                                      out_bank[n][:, 0:w], ALU.mult, ALU.add))
                        for at in range(col, col + w, size):
                            last = dve.bn_stats(stats[:, t, at // size, :], total[:, t, at:at + size])
                        link(last)
                dve.bn_aggr(moments[:, t, :], stats[:, t, 0:D_MODEL // size, :].rearrange("p n s -> p (n s)")).then_inc(mom_ok, 1)
                dve.wait_ge(mom_ok, t + 1)
                if t == 0:
                    centre(0).then_inc(centred, 1)
                    centre(1).then_inc(centred, 1)
            centre(2).then_inc(centred, 1)
            centre(3)
            link(centre(4))
            dve.wait_ge(rstd_ok, TT)
            for t, cols in stretches[3:]:
                dve.scalar_tensor_tensor(total[:, t, cols], total[:, t, cols], rstd[:, t, 1:2], bias[:, cols],
                                         ALU.mult, ALU.add).then_inc(fin_dve, 1)

        @block.tensor
        def _(pe):
            def project_tile(c, t, kt):
                w = width(c)
                piece, j, tok = (2 * c + kt // 4) % HL, kt % 4, slice(t * P, (t + 1) * P)
                pe.matmul(acc[t][:, 0:w], x_hi[:, kt, tok], w_hi[:, piece, j, 0:w], start=(kt == 0), stop=False)
                pe.matmul(acc[t][:, 0:w], x_hi[:, kt, tok], w_lo[:, piece, j, 0:w], start=False, stop=False)
                return pe.matmul(acc[t][:, 0:w], x_lo[:, kt, tok], w_hi[:, piece, j, 0:w], start=False, stop=(kt == KT - 1))

            def project_first(s):
                for kt in ((2 * s, 2 * s + 1) if s < 2 else range(4, 8)):
                    for n, (kt0, _) in enumerate(FIRST):
                        if kt == kt0 and s < 3:
                            pe.wait_ge(x_lo_ok, n + 1)
                            if n < len(FIRST) - 1:
                                pe.wait_ge(first_lo, n + 1)
                            else:
                                pe.wait_ge(lo_ok, 4)
                    for t in (range(TT) if s < 2 else (s - 2,)):
                        last = project_tile(C_KV, t, kt)
                last.then_inc(group_done, 1)

            def project(s):
                c, t, k = s // 4, s % 4 // 2, s % 2
                n = 2 * c + t
                if k == 0:
                    old = (n - 2) // 2
                    if old in (C_NV, C_MV):
                        pe.wait_ge(v_ok, 2 * (old == C_MV) + t + 1)
                    elif old == C_NZ:
                        pe.wait_ge(z_read, t + 1)
                    else:
                        pe.wait_ge(acc_read, sections_before(old) + t + 1)
                for kt in range(4 * k, 4 * k + 4):
                    if t == 0 and kt % 2 == 0:
                        pe.wait_ge(lo_ok, 4 * c + kt // 2 + 1)
                    last = project_tile(c, t, kt)
                last.then_inc(group_done, 1)

            def transposes(name, blocks, n=4):
                wait_turn_free(pe, name)
                for m in range(n):
                    last = pe.transpose(turn_bank(name)[:, m * P:(m + 1) * P], blocks(m), ident)
                last.then_inc(turn_full, 1)

            def section_turn(name, tok, t, ropes):
                pe.wait_ge(rope_ok, ropes)
                transposes(name, lambda m: tok[:, t, m * P:(m + 1) * P])

            def gate_turn(name, z, t, reads):
                pe.wait_ge(z_read, reads)
                transposes(name, lambda m: z[:, t, m * P:(m + 1) * P])

            def unit_scores(i):
                g, kind = unit_of(i)
                if i >= 2:
                    pe.wait_ge(probs_ok, i - 1)
                bank = scores[i % 2]
                q_tok_tile = slice(P, SEQ) if kind < 2 else slice(0, P)
                if g < 4:
                    work = [(q_st[:, 2 * g + h, q_tok_tile],
                             [k[:, g // 2, kind, :] if kind < 2 else k[:, g // 2, :, 0:P] for k in (k_hi, k_lo)])
                            for h in range(2)]
                else:
                    first = 4 * (g - 4) + (2 * kind if kind < 2 else 0)
                    work = [(qm_st[:, head, q_tok_tile], [k[:, head, 0:SEQ if kind < 2 else P] for k in (km_hi, km_lo)])
                            for head in range(first, first + (2 if kind < 2 else 4))]
                w = CH // len(work)
                for n, (q, parts) in enumerate(work):
                    for part, keys in enumerate(parts):
                        dst = bank[:, n * w:(n + 1) * w]
                        if len(keys.shape) == 3:
                            dst = dst.rearrange("p (b k) -> p b k", b=2)
                        pe.matmul(dst, q, keys, start=(n == 0 and part == 0), stop=False, skip_group_check=True)
                tiles = bank[:, :].rearrange("p (n k) -> p n k", k=P)
                causal = causal_bf[:, :].unsqueeze(1).broadcast_to((P, 2, P))
                if kind < 2:
                    last = pe.matmul(tiles[:, 1::2, :], ident_bf[:, :], causal, start=False, stop=True,
                                     skip_group_check=True)
                else:
                    for n in range(2):
                        last = pe.matmul(tiles[:, 2 * n:2 * n + 2, :], ident_bf[:, :], causal, start=False,
                                         stop=(n == 1), skip_group_check=True)
                last.then_inc(scores_ok, 1)

            def unit_turn(i):
                pe.wait_ge(scaled_ok, i + 1)
                transposes(f"p{i}", lambda m: probs[:, i % 2, m * P:(m + 1) * P])

            def unit_heads(i):
                g, kind = unit_of(i)
                pe.wait_ge(turn_dve, dve_turns(f"p{i}"))
                if g < 4:
                    if kind == 0 and g >= 2:
                        pe.wait_ge(heads_read, g - 1)
                    out_h = heads[g % 2][:, :].rearrange("p (h q) -> p h q", h=2)
                    passes = [(part, x) for x in range(2) for part in (pT_hi, pT_lo)]
                    for n, (part, x) in enumerate(passes):
                        p4 = part[:, i % 2, :, :].rearrange("p (h x) q -> p h x q", h=2)[:, :, x, :]
                        branch, tile = (kind, x) if kind < 2 else (x, 0)
                        last = pe.matmul(out_h[:, :, P:SEQ] if kind < 2 else out_h[:, :, 0:P],
                                         v_st[:, tile, branch * GROUPS + g // 2, :], p4,
                                         start=(n == 0 and kind != 1), stop=(n == 3 and kind != 0), skip_group_check=True)
                else:
                    if kind < 2:
                        pe.wait_ge(heads_read, 2 * g - 4 + kind - 1)
                    first = 2 * (g - 4) + (kind if kind < 2 else 0)
                    tiles = 2 if kind < 2 else 1
                    for h in range(2 if kind < 2 else 4):
                        pair, side = first + h // 2, h % 2
                        for kt in range(tiles):
                            for n, part in enumerate((pT_hi, pT_lo)):
                                last = pe.matmul(heads[pair % 2][:, side * SEQ + (P if kind < 2 else 0):
                                                                 side * SEQ + (SEQ if kind < 2 else P)],
                                                 vm_st[:, kt, 2 * pair + side, :], part[:, i % 2, h * tiles + kt, :],
                                                 start=(side == 0 and kt == 0 and n == 0),
                                                 stop=(side == 1 and kt == tiles - 1 and n == 1), skip_group_check=True)
                last.then_inc(heads_ok, 1)

            def hidden(kind, name):
                wait_turn_free(pe, name)
                pe.wait_ge(packed, 8 * kind + 8)
                for i in range(CKT):
                    if i % 8 == 0:
                        n = PIECES.index((("fk", "fv")[kind], kind, i // 8))
                        wait_piece(pe, PIECES[n])
                    j = i % 4
                    w = raw[:, n % RAW, (i % 8) * CMP_HIDDEN:(i % 8 + 1) * CMP_HIDDEN]
                    last = pe.matmul(turn_bank(name)[32 * j:32 * j + 32, 0:CMP_HIDDEN], cmp_in[:, kind, i, :], w,
                                     start=(i < 4), stop=(i >= CKT - 4))
                    if i == CKT // 2 - 1:
                        last.then_inc(hid_read, 1)
                last.then_inc(turn_full, 1)

            def compressed_heads(half):
                wait_turn_free(pe, f"oc{half}")
                pe.wait_ge(turn_act, act_turns("cp"))
                for m in range(2):
                    last = pe.matmul(turn_bank(f"oc{half}")[:, m * SEQ:(m + 1) * SEQ], vc_B[:, 2 * half + m, :], cmp_pT[:, :],
                                     start=True, stop=True)
                last.then_inc(turn_full, 1)

            pe.wait_ge(idle_ok, 1)
            for n in range(WARM_UP):
                pe.matmul(heads[0][:, 0:P], hid_parts[:, 0, 0:P], hid_parts[:, 0, 0:P], start=True, stop=True)
            for s in range(STEPS):
                i = s - UNIT0
                if s < 4:
                    project_first(s)
                else:
                    project(s)
                if i == 0:
                    pe.wait_ge(bf_ok, 1)
                    pe.wait_ge(turn_dve, dve_turns("qrot1"))
                if i == 3:
                    pe.wait_ge(v_ok, 2)
                if i == 12:
                    pe.wait_ge(turn_dve, dve_turns("mq1"))
                    pe.wait_ge(km_in[0], 16)
                    pe.wait_ge(km_in[1], 16)
                if i == 15:
                    pe.wait_ge(v_ok, 4)
                if 0 <= i < UNITS:
                    unit_scores(i)
                if 0 <= i - 2 < UNITS:
                    unit_turn(i - 2)
                if 0 <= i - 3 < UNITS:
                    unit_heads(i - 3)
                if s == 4:
                    pe.wait_ge(k_in, 16)
                    section_turn("kv0", keys_tok, 0, 1)
                if s == 5:
                    section_turn("kv1", keys_tok, 1, 2)
                if s in (6, 8):
                    t = (s - 6) // 2
                    pe.wait_ge(acc_read, 3 + t)
                    transposes(f"qraw{t}", lambda m: q_tok[:, t, m * P:(m + 1) * P])
                if s == 9:
                    section_turn("qrot0", q_tok, 0, 3)
                if s == 11:
                    section_turn("qrot1", q_tok, 1, 4)
                if s == 11:
                    hidden(0, "hk")
                if s == 12:
                    hidden(1, "hv")
                if s == 13:
                    wait_turn_free(pe, "hT")
                    pe.wait_ge(turn_dve, dve_turns("hv"))
                    pe.wait_ge(b1_in, 16)
                    pe.wait_ge(zero_ok, 3)
                    for kind in range(2):
                        for half in range(2):
                            cols = slice(half * P, (half + 1) * P)
                            dst = turn_bank("hT")[:, (2 * kind + half) * P:(2 * kind + half + 1) * P]
                            pe.matmul(dst, hid_parts[:, kind, cols], const(K_SEL), start=True, stop=False)
                            last = pe.matmul(dst, b1_sb[:, kind, cols], ones_sb[:, :], start=False, stop=True)
                    last.then_inc(turn_full, 1)
                if s == 14:
                    wait_turn_free(pe, "kcvc")
                    pe.wait_ge(turn_dve, dve_turns("hT"))
                    pe.wait_ge(w2k_in, 16)
                    pe.wait_ge(w2v_in, 16)
                    for copy in range(2):
                        rows = slice(64 * copy, 64 * copy + 64)
                        for half in range(2):
                            blocks = hid[:, 0, half, :].rearrange("p (g n) -> p g n", g=GROUPS)[:, :, 0:CPAD]
                            pe.matmul(turn_bank("kcvc")[rows, 0:GROUPS * CPAD].rearrange("p (g n) -> p g n", g=GROUPS),
                                      w2k_sb[:, half, :], blocks, start=(half == 0), stop=(half == 1))
                    for half in range(2):
                        last = pe.matmul(turn_bank("kcvc")[:, 64:P], hid[:, 1, half, :], w2v_sb[:, half, :],
                                         start=(half == 0), stop=(half == 1))
                    last.then_inc(turn_full, 1)
                if s == 15:
                    wait_turn_free(pe, "cs")
                    pe.wait_ge(turn_dve, dve_turns("kcvc"))
                    for t in range(TT):
                        for m in range(4):
                            at = t * P + m * 2 * CPAD
                            pe.matmul(turn_bank("cs")[:, at:at + 2 * CPAD], qraw_T[:, m, t * P:(t + 1) * P],
                                      kc_B[:, m // 2, :], start=(t == 0 and m == 0), stop=False, skip_group_check=True)
                    last = pe.matmul(turn_bank("cs")[:, 0:TT * P], ident_bf[:, :], cmask_bf[:, :, :].rearrange("p t n -> p (t n)"),
                                     start=False, stop=True, skip_group_check=True)
                    last.then_inc(turn_full, 1)
                if s == 17:
                    section_turn("mk0", keys_tok, 0, 5)
                if s == 24:
                    pe.wait_ge(cmp_pok, 1)
                    transposes("cp", lambda m: cmp_p[:, m, :], TT)
                if s == 19:
                    section_turn("mk1", keys_tok, 1, 6)
                if s == 20:
                    section_turn("mq0", q_tok, 0, 7)
                if s == 22:
                    section_turn("mq1", q_tok, 1, 8)
                if s == 26:
                    compressed_heads(0)
                if s in (27, 29):
                    gate_turn(f"zn{(s - 27) // 2}", keys_tok, (s - 27) // 2, (s - 27) // 2 + 1)
                if s == 28:
                    compressed_heads(1)
                if s == 31:
                    gate_turn("zm0", q_tok, 0, 3)

            def out_half(c, part):
                t, col, w = OUT_PARTS[part]
                first, cols = 2 * (c - C_OA) + col // CH, slice(col % CH, col % CH + w)
                parts, bank, tok = y_parts[c - C_OA], out_bank[part][:, 0:w], slice(t * P, (t + 1) * P)
                piece = (2 * C_OA + first) % HL
                for j in range(4):
                    if j % 2 == 0:
                        pe.wait_ge(lo_ok, 4 * C_OA + 2 * first + j // 2 + 1)
                    pe.matmul(bank, parts[:, j, tok], w_hi[:, piece, j, cols], start=(c == C_OA and j == 0), stop=False)
                    pe.matmul(bank, parts[:, j, tok], w_lo[:, piece, j, cols], start=False, stop=False)
                    last = pe.matmul(bank, parts[:, 4 + j, tok], w_hi[:, piece, j, cols], start=False,
                                     stop=(c == C_OB and j == 3))
                last.then_inc(group_done if c == C_OA else out_ok, 1)

            pe.wait_ge(z_read, 3)
            pe.wait_ge(y_lo_ok, 1)
            out_half(C_OA, 0)
            unit_heads(17)
            gate_turn("zm1", q_tok, 1, 4)
            pe.wait_ge(probs_ok, UNITS)
            pe.wait_ge(y_lo_ok, 2)
            out_half(C_OA, 2)
            out_half(C_OA, 1)
            out_half(C_OA, 3)
            pe.wait_ge(turn_act, act_turns("zm0"))
            out_half(C_OA, 4)
            for part, (t, _, _) in enumerate(OUT_PARTS):
                pe.wait_ge(y_lo_ok, 3 + t)
                out_half(C_OB, part)


def last_use(piece):
    c, k = piece // 2, piece % 2
    if c == C_KV:
        return 2 * k + 2
    if c < C_OA:
        return 4 * c + 2 + k + 1
    return STEPS + (2, len(OUT_PARTS))[k]


def splits_in(s):
    c = s // 4 + 1
    return {0: [4 * c], 1: [4 * c + 1], 2: [], 3: [4 * c + 2, 4 * c + 3]}[s % 4]


def low_splits_in(s):
    c = s // 4 + 1
    return {0: [4 * c - 1] if s else [], 1: [4 * c], 2: [4 * c + 1], 3: []}[s % 4]


def kernel(x, w_in, cmp_pos_k, cmp_w1_k, cmp_b1_k, cmp_w2_k,
           cmp_pos_v, cmp_w1_v, cmp_b1_v, cmp_w2_v, w_out, ln_gain, ln_bias):
    import concourse.bacc as bacc
    from concourse.bass_utils import run_bass_kernel_spmd

    a = lambda v: np.asarray(v)
    x, w, wo = a(x)[0], a(w_in)[0], a(w_out)[0]
    sizes = [D_NSA] + [KV] * 6 + [GATES, D_NSA] + [D_MOBA] * 4
    at = np.cumsum([0] + sizes)
    q, kc, vc, ks, vs, kw, vw, ga, z, mq, mk, mv, mz = (w[:, at[n]:at[n + 1]] for n in range(13))

    def pieces(m):
        return m.reshape(2, 4, P, -1).transpose(0, 2, 1, 3).reshape(2, P, -1)

    ga = ga.reshape(D_MODEL, GROUPS * REPS, 3).transpose(0, 2, 1).reshape(D_MODEL, GATES)

    def out_pieces(m):
        return m.reshape(4, P, 2, CH).transpose(2, 1, 0, 3).reshape(2, P, 4 * CH)

    chunks = [np.concatenate([kc, vc, ks, kw], 1), q, mk, mq, mv, z, mz]
    w_full = np.concatenate([pieces(m) for m in chunks] + [out_pieces(wo[:D_NSA]), out_pieces(wo[D_NSA:])])
    w_nv = pieces(np.concatenate([vs, vw, ga], 1))
    w1 = np.stack([a(m)[0].reshape(2, CKT // 2, P, CMP_HIDDEN).transpose(0, 2, 1, 3).reshape(2, P, PIECE)
                   for m in (cmp_w1_k, cmp_w1_v)])
    pos = np.stack([a(m)[0].reshape(CKT, 2, HEAD_DIM).transpose(2, 1, 0) for m in (cmp_pos_k, cmp_pos_v)], 1)
    pos = np.concatenate([pos, pos], 0)
    b1 = np.stack([a(cmp_b1_k)[0], a(cmp_b1_v)[0]])[None]
    w2k = a(cmp_w2_k)[0].reshape(2, P, HEAD_DIM).transpose(1, 0, 2)
    w2v = a(cmp_w2_v)[0].reshape(2, P, HEAD_DIM).transpose(1, 0, 2)
    xT = x.T.reshape(KT, P, SEQ).transpose(1, 0, 2).reshape(P, KT * SEQ)
    x_res = x.reshape(TT, P, D_MODEL).transpose(1, 0, 2).reshape(P, TT * D_MODEL)
    gain_bias = np.concatenate([a(ln_gain)[0], a(ln_bias)[0]])

    nc = bacc.Bacc("TRN2", target_bir_lowering=False, num_devices=1)
    arrays, args = {}, []
    for name, v in (("xT", xT), ("w_full", w_full), ("w_nv", w_nv), ("w1", w1), ("kmat", constants()), ("pos", pos),
                    ("b1", b1), ("w2k", w2k), ("w2v", w2v), ("x_res", x_res), ("gain_bias", gain_bias)):
        v = np.ascontiguousarray(v)
        arrays[f"in_{name}"] = v
        args.append(nc.dram_tensor(f"in_{name}", v.shape, mybir.dt.from_np(v.dtype), kind="ExternalInput").ap())
    out = nc.dram_tensor("out_0", (SEQ, D_MODEL), mybir.dt.float32, kind="ExternalOutput").ap()
    build(nc, *args, out)
    r = run_bass_kernel_spmd(nc, [arrays], core_ids=[0])
    return r.results[0]["out_0"].reshape(1, SEQ, D_MODEL)
```

```python
import numpy as np
import concourse.bass as bass
from concourse import mybir
from contextlib import ExitStack

P = 128
SEQ, D_MODEL, HEAD_DIM = 256, 1024, 64
TT = SEQ // P
KT = D_MODEL // P
GROUPS, REPS = 2, 4
D_NSA, D_MOBA = 512, 512
KV = GROUPS * HEAD_DIM
CH = 512
GATES = 3 * GROUPS * REPS
NARROW = 2 * KV + GATES
ROPE, HALF = HEAD_DIM // 4, HEAD_DIM // 8
ROPE_THETA = 500000.0
CMP_BLOCK, CMP_STRIDE, CMP_HIDDEN = 32, 16, 256
NCMP = SEQ // CMP_STRIDE - 1
CPAD = 16
CKT = CMP_BLOCK * HEAD_DIM // P
LN_EPS = 1e-5
ALPHA = 2.0 ** 0.25
NEG = -1e30
SCALE = HEAD_DIM ** -0.5

C_KV, C_NQ, C_NV, C_MK, C_MQ, C_MV, C_NZ, C_MZ, C_OA, C_OB = range(10)
TRANSPOSED = (C_KV, C_NQ, C_MK, C_MQ, C_NZ, C_MZ)
STEPS = 4 * 8
UNIT0 = 12
UNITS, NSA_UNITS = 18, 12
RAW, HL, PIECE = 5, 3, 4 * CH

PIECES = ([("x", 0, 0)] + [("w", c, k) for c in (C_KV, C_NQ) for k in (0, 1)]
          + [("w", c, k) for c in (C_NV, C_MK) for k in (0, 1)]
          + [("fk", 0, 0), ("fk", 0, 1), ("fv", 1, 0), ("fv", 1, 1)]
          + [("w", c, k) for c in (C_MQ, C_MV, C_NZ, C_MZ, C_OA, C_OB) for k in (0, 1)]
          + [("res", 0, 0), ("gb", 0, 0)])

WARM_UP = 8

OUT_PARTS = [(0, 0, CH), (0, CH, CH), (1, 0, CH), (1, CH, CH // 2), (1, CH + CH // 2, CH // 2)]
SHARE, FORE = 320, 640

TURNS = [("hk", "dve"), ("hv", "dve"), ("p0", "both"), ("hT", "both"),
         ("p1", "both"), ("kcvc", "dve"), ("p2", "both"), ("cs", "dve"),
         ("p3", "both"), ("p4", "both"), ("p5", "both"), ("p6", "both"), ("p7", "both"), ("p8", "both"), ("p9", "both"),
         ("p10", "both"), ("cp", "act"), ("p11", "both"), ("p12", "both"), ("oc0", "dve"), ("p13", "both"),
         ("p14", "both"), ("oc1", "dve"), ("p15", "both"), ("p16", "both"), ("p17", "both")]
TURN_AT = {name: n for n, (name, _) in enumerate(TURNS)}


def act_turns(name):
    return sum(who != "dve" for _, who in TURNS[:TURN_AT[name] + 1])


def dve_turns(name):
    return sum(who != "act" for _, who in TURNS[:TURN_AT[name] + 1])


def unit_of(i):
    return i // 3, i % 3 if i < NSA_UNITS else (0, 2, 1)[i % 3]


def part_slot(i):
    return i % 2 if i < NSA_UNITS else (1, 0, 1)[i % 3]


def heads_after(i):
    return i + 1 if i < NSA_UNITS else NSA_UNITS + 2 * (i // 3 - 4) + i % 3


SECTIONS = [(C_KV, 1), (C_NQ, 0), (C_NQ, 1), (C_MK, 0), (C_MK, 1), (C_MQ, 0), (C_MQ, 1)]


def width(c):
    return NARROW if c == C_NV else CH


def sections_before(c):
    return 2 * (C_KV, C_NQ, C_MK, C_MQ).index(c)


def units_before(m):
    return 3 * m + 3 if m < 4 else NSA_UNITS + m - 3


K_IDENT, K_SEL, K_CVALID, K_BLOCK, K_CAUSAL, K_CMASK = range(6)
K_SIZES = [P, P, TT * CPAD, GROUPS * REPS, P, TT * P]
K_AT = [sum(K_SIZES[:n]) for n in range(len(K_SIZES) + 1)]
K_KEPT = K_AT[K_CAUSAL]


HEAD_ORDER = [*range(0, HALF), *range(ROPE, 40), *range(HALF, ROPE), *range(40, HEAD_DIM)]


def rope_rows():
    k = np.stack([np.ones((P, SEQ), np.float32), np.zeros((P, SEQ), np.float32)], 1)
    inv = np.float32(ROPE_THETA) ** (-np.arange(0, ROPE, 2, dtype=np.float32) / np.float32(ROPE))
    ang = inv[:, None].astype(np.float32) * np.arange(SEQ, dtype=np.float32)[None, :]
    for q in range(4):
        rows = slice(32 * q, 32 * q + HALF)
        k[rows, 0], k[rows, 1] = np.cos(ang), np.sin(ang) * np.float32(1 if q % 2 else -1)
    return k


def constants():
    k = np.zeros((P, K_AT[-1]), np.float32)
    at = lambda n: k[:, K_AT[n]:K_AT[n + 1]]
    row = np.arange(P)
    at(K_IDENT)[:] = np.eye(P)
    at(K_SEL)[:] = ((row[:, None] % 32 // CPAD == row[None, :] // (REPS * CPAD))
                    & (row[:, None] % CPAD == row[None, :] % CPAD))
    at(K_CAUSAL)[:] = np.where(row[None, :] > row[:, None], NEG, 0.0)
    c = np.arange(CPAD)
    for t in range(TT):
        ok = (c[None, :] * CMP_STRIDE + CMP_BLOCK - 1 <= (t * P + row)[:, None]) & (c[None, :] < NCMP)
        at(K_CVALID)[:, t * CPAD:(t + 1) * CPAD] = ok
        at(K_CMASK)[:, t * P:(t + 1) * P] = np.tile(np.where(ok, 0.0, NEG), (1, P // CPAD))
    at(K_BLOCK)[:] = 0.5 * (row[:, None] // CPAD == np.arange(P // CPAD)[None, :])
    return k


def build(nc, xT, w_full, w_nv, w1, kmat, ropeT, pos, b1, w2k, w2v, x_res, gain_bias, out):
    f32, f32r, bf16 = mybir.dt.float32, mybir.dt.float32r, mybir.dt.bfloat16
    ALU, ACT, AX = mybir.AluOpType, mybir.ActivationFunctionType, mybir.AxisListType
    ctx = ExitStack()
    with ctx:
        def sb(name, shape, dt=f32):
            return ctx.enter_context(nc.sbuf_tensor(name, shape, dt))

        def ps(name):
            return ctx.enter_context(nc.psum_tensor(name, [P, CH], f32))

        def sem(name):
            return ctx.enter_context(nc.semaphore(name))

        raw = sb("raw", [P, RAW, PIECE])
        w_hi = sb("w_hi", [P, HL, 4, CH], f32r)
        w_lo = sb("w_lo", [P, HL, 4, CH], f32r)
        x_hi = sb("x_hi", [P, KT, SEQ], f32r)
        x_lo = sb("x_lo", [P, KT, SEQ], f32r)
        k_sb = sb("k_sb", [P, K_KEPT])
        ident_bf = sb("ident_bf", [P, P], bf16)
        causal_bf = sb("causal_bf", [P, P], bf16)
        cmask_bf = sb("cmask_bf", [P, TT, P], bf16)
        pos_sb = sb("pos_sb", [P, 2, 2, CKT])
        ones_sb = sb("ones_sb", [1, P])
        w2k_sb = sb("w2k_sb", [P, 2, HEAD_DIM])
        w2v_sb = sb("w2v_sb", [P, 2, HEAD_DIM])
        keys = sb("keys", [P, 2, CH])
        queries = sb("queries", [P, 2, CH])
        qraw_T = sb("qraw_T", [P, 4, SEQ])
        q_st = sb("q_st", [P, 8, SEQ], f32r)
        qm_st = sb("qm_st", [P, 8, SEQ], f32r)
        k_hi = sb("k_hi", [P, GROUPS, 2, SEQ], f32r)
        k_lo = sb("k_lo", [P, GROUPS, 2, SEQ], f32r)
        km_hi = sb("km_hi", [P, 8, SEQ], f32r)
        km_lo = sb("km_lo", [P, 8, SEQ], f32r)
        kvc_T = sb("kvc_T", [P, 2, SEQ])
        cmp_in = sb("cmp_in", [P, 2, CKT, 2 * CPAD])
        hid_parts = sb("hid_parts", [P, 2, CMP_HIDDEN])
        hid = sb("hid", [P, 2, 2, P])
        b1_sb = hid[0:1, :, :, :].rearrange("p a b n -> p a (b n)")
        kc_B = sb("kc_B", [P, GROUPS, 2 * CPAD])
        vc_B = sb("vc_B", [P, 4, P])
        cmp_p = sb("cmp_p", [P, TT, P])
        cmp_stat = sb("cmp_stat", [P, 3, TT, 8])
        cmp_pT = sb("cmp_pT", [P, SEQ])
        v_st = sb("v_st", [P, TT, 2 * GROUPS, P], f32r)
        vm_st = sb("vm_st", [P, TT, 8, P], f32r)
        gates = sb("gates", [P, TT, GATES])
        probs = sb("probs", [P, 2, CH])
        pT_hi = sb("pT_hi", [P, 2, 4, P], f32r)
        pT_lo = sb("pT_lo", [P, 2, 4, P], f32r)
        masks = probs[:, 0, 0:3 * P]
        neg_max = sb("neg_max", [P, 2, 4])
        row_sum = sb("row_sum", [P, 2, 4])
        inverse = sb("inverse", [P, 4])
        weight = sb("weight", [P, 2, 4])
        o_T = sb("o_T", [P, 8, SEQ])
        stats = sb("stats", [P, TT, 4, 6])
        moments = sb("moments", [P, TT, 2])
        rstd = sb("rstd", [P, TT, 3])
        zT = [qraw_T[:, :, :],
              cmp_in[:, :, :, :].rearrange("p a b c -> p (a b c)").rearrange("p (m t) -> p m t", m=4)]
        rope_T = o_T[:, 6:8, :]
        nsa_partner = o_T[:, 0:4, :].rearrange("p (n m) t -> p n (m t)", n=2)
        moba_partner = cmp_in[:, :, :, :].rearrange("p a b c -> p a (b c)")

        def partner_of(section):
            return (nsa_partner if section < 3 else moba_partner)[:, SECTIONS[section][1], :]

        def unrotated(section):
            c, b = SECTIONS[section]
            if c == C_NQ:
                return qraw_T[:, 2 * b:2 * b + 2, :].rearrange("p m t -> p (m t)")
            return (queries if c == C_MQ else keys)[:, b, :]

        def rotated(section):
            c, b = SECTIONS[section]
            return (queries if c in (C_NQ, C_MQ) else keys)[:, b, :]

        y_parts = [q_st, qm_st]

        acc = [ps(f"acc{n}") for n in range(2)]
        scores = [ps(f"scores{n}") for n in range(2)]
        turn = [ps(f"turn{n}") for n in range(2)]
        heads = [ps(f"heads{n}") for n in range(2)]

        raw_in = [sem(f"raw_in{n}") for n in range(RAW)]
        x_in = [sem(f"x_in{kt}") for kt in range(KT)]
        w_in = [sem(f"w_in{kt}") for kt in range(KT)]
        nq_in = [sem(f"nq_in{n}") for n in range(4)]
        first_hi, first_lo = sem("first_hi"), sem("first_lo")
        k_in, mask_in, pos_in, b1_in, w2k_in, w2v_in = (sem(n) for n in ("k_in", "mask_in", "pos_in", "b1_in", "w2k_in", "w2v_in"))
        x_hi_ok, x_lo_ok = sem("x_hi_ok"), sem("x_lo_ok")
        hi_ok, lo_ok = sem("hi_ok"), sem("lo_ok")
        bf_ok = sem("bf_ok")
        idle_ok = sem("idle_ok")
        zero_ok = sem("zero_ok")
        group_done = sem("group_done")
        acc_read = sem("acc_read")
        z_tanh, z_read = sem("z_tanh"), sem("z_read")
        rope_a, rope_ok = sem("rope_a"), sem("rope_ok")
        turn_full = sem("turn_full")
        turn_act, turn_dve = sem("turn_act"), sem("turn_dve")
        ropeT_in = sem("ropeT_in")
        swap_in = [sem(f"swap_in{n}") for n in range(len(SECTIONS))]
        part_hi, part_lo = sem("part_hi"), sem("part_lo")
        km_in = [sem(f"km_in{n}") for n in range(2)]
        packed = sem("packed")
        hid_read = sem("hid_read")
        scores_ok, max_ok, probs_ok = sem("scores_ok"), sem("max_ok"), sem("probs_ok")
        weight_ok, scaled_ok = sem("weight_ok"), sem("scaled_ok")
        heads_ok, heads_hi, heads_read = sem("heads_ok"), sem("heads_hi"), sem("heads_read")
        v_hi_ok, v_ok = sem("v_hi_ok"), sem("v_ok")
        link_done = sem("link_done")
        cmp_shift, cmp_exp, cmp_pok = sem("cmp_shift"), sem("cmp_exp"), sem("cmp_pok")
        y_ok, y_hi_ok, y_lo_ok = sem("y_ok"), sem("y_hi_ok"), sem("y_lo_ok")
        out_ok = sem("out_ok")
        total_ok, stats_ok = sem("total_ok"), sem("stats_ok")
        mom_ok, eps_ok, rstd_ok = sem("mom_ok"), sem("eps_ok"), sem("rstd_ok")
        centred, spread = sem("centred"), sem("spread")
        fin_pool, fin_dve = sem("fin_pool"), sem("fin_dve")
        stored = [sem(f"stored{n}") for n in range(5)]

        sections_at = [10, 12, 14, 17, 20, 22, 25]
        const = lambda n: k_sb[:, K_AT[n]:K_AT[n + 1]]
        ident = const(K_IDENT)
        out_bank = [acc[0], scores[0], acc[1], scores[1], turn[TURN_AT["p16"] % 2]]
        stretches = [(0, slice(0, CH)), (0, slice(CH, D_MODEL)), (1, slice(0, SHARE)),
                     (1, slice(SHARE, FORE)), (1, slice(FORE, D_MODEL))]
        res = PIECES.index(("res", 0, 0))
        gb = PIECES.index(("gb", 0, 0))
        x_tok = raw[:, res % RAW, :].rearrange("p (t n) -> p t n", t=TT)
        total = raw[:, (gb - 3) % RAW, :].rearrange("p (t n) -> p t n", t=TT)
        gain = raw[:, gb % RAW, 0:D_MODEL]
        bias = raw[:, gb % RAW, D_MODEL:2 * D_MODEL]

        def wait_piece(eng, piece):
            n = PIECES.index(piece)
            eng.wait_ge(raw_in[n % RAW], 16 * (n // RAW))

        def wait_turn_free(eng, name):
            n = TURN_AT[name]
            if n >= 2:
                old, who = TURNS[n - 2]
                if who == "act":
                    eng.wait_ge(turn_act, act_turns(old))
                else:
                    eng.wait_ge(turn_dve, dve_turns(old))

        def wait_turn(eng, name):
            eng.wait_ge(turn_full, TURN_AT[name] + 1)

        def turn_bank(name):
            return turn[TURN_AT[name] % 2]

        block = ctx.enter_context(nc.Block())

        @block.sync
        def _(sp):
            def swap(section):
                c, b = SECTIONS[section]
                sp.wait_ge(acc_read, sections_before(c) + b + 1)
                if section == 0:
                    sp.wait_ge(zero_ok, 4)
                if section == 2:
                    sp.wait_ge(rope_ok, 1)
                if section >= 5:
                    sp.wait_ge(rope_ok, section - 1)
                for q in range(4):
                    to = 32 * (q + 1 if q % 2 == 0 else q - 1)
                    sp.dma_start(partner_of(section)[to:to + HALF], unrotated(section)[32 * q:32 * q + HALF]).then_inc(swap_in[section], 16)

            for kt in range(KT):
                part = slice(kt * SEQ, (kt + 1) * SEQ)
                sp.dma_start(raw[:, 0, part], xT[:, part]).then_inc(x_in[kt], 16)
                part = slice(kt % 4 * CH, (kt % 4 + 1) * CH)
                sp.dma_start(raw[:, 1 + kt // 4, part], w_full[kt // 4][:, part]).then_inc(w_in[kt], 16)
            for u in range(4):
                part = slice(u % 2 * 2 * CH, (u % 2 + 1) * 2 * CH)
                sp.dma_start(raw[:, 3 + u // 2, part], w_full[2 * C_NQ + u // 2][:, part]).then_inc(nq_in[u], 16)
                if u == 1:
                    sp.dma_start(k_sb[:, :], kmat[:, 0:K_KEPT]).then_inc(k_in, 16)
            sp.dma_start(pos_sb[:, :, :, :], pos).then_inc(pos_in, 16)
            sp.dma_start(masks, kmat[:, K_KEPT:]).then_inc(mask_in, 16)
            sp.dma_start(rope_T, ropeT).then_inc(ropeT_in, 16)
            sp.dma_start(b1_sb, b1).then_inc(b1_in, 16)
            sp.dma_start(w2k_sb[:, :, :], w2k).then_inc(w2k_in, 16)
            sp.dma_start(w2v_sb[:, :, :], w2v).then_inc(w2v_in, 16)
            before = [("w", C_MK, 0), ("fk", 0, 0), ("fv", 1, 0), ("w", C_NZ, 1), ("w", C_MZ, 0), ("w", C_MZ, 1), ("w", C_OA, 0)]
            for n, (kind, c, k) in enumerate(PIECES):
                if n < RAW:
                    continue
                old, oc, ok = PIECES[n - RAW]
                if old == "x":
                    sp.wait_ge(x_lo_ok, KT)
                elif old == "w":
                    sp.wait_ge(lo_ok, 4 * oc + 2 * ok + 2)
                elif ok == 0:
                    sp.wait_ge(hid_read, oc + 1)
                else:
                    wait_turn(sp, ("hk", "hv")[oc])
                if PIECES[n] in before:
                    section = before.index(PIECES[n])
                    if section == 3:
                        wait_turn(sp, "hv")
                    swap(section)
                dst = raw[:, n % RAW, :]
                if kind == "x":
                    src = xT
                elif kind == "w" and c == C_NV:
                    dst, src = raw[:, n % RAW, 0:4 * NARROW], w_nv[k]
                elif kind == "w":
                    src = w_full[2 * (c - (c > C_NV)) + k]
                elif kind == "res":
                    src = x_res
                elif kind == "gb":
                    src = gain_bias.partition_broadcast(P)
                else:
                    src = w1[c, k]
                sp.dma_start(dst, src).then_inc(raw_in[n % RAW], 16)
            for n in (0, 1, 3, 2, 4):
                t, cols = stretches[n]
                if n < 3:
                    sp.wait_ge(fin_pool, n + 1)
                else:
                    sp.wait_ge(fin_dve, n - 2)
                sp.dma_start(out[t * P:(t + 1) * P, cols], total[:, t, cols]).then_inc(stored[n], 16)
            for s in stored:
                sp.wait_ge(s, 16)

        @block.gpsimd
        def _(pool):
            pool.memset(hid_parts[:, 0, 0:P], 0.0).then_inc(idle_ok, 1)
            pool.memset(cmp_in[:, :, :, :], 0.0).then_inc(zero_ok, 1)
            pool.memset(kc_B[:, :, :], 0.0).then_inc(zero_ok, 1)
            pool.memset(ones_sb[:, :], 1.0).then_inc(zero_ok, 1)
            pool.memset(nsa_partner, 0.0).then_inc(zero_ok, 1)
            pool.memset(rstd[:, :, 2:3], -0.5).then_inc(eps_ok, 1)

            def rope(section):
                pairs = lambda x: x.rearrange("p (m t) -> p m t", m=2)
                v, turned, part = pairs(unrotated(section)), pairs(rotated(section)), pairs(partner_of(section))
                factor = lambda n: rope_T[:, n, :].unsqueeze(1).broadcast_to((P, 2, SEQ))
                pool.wait_ge(ropeT_in, 16)
                pool.wait_ge(swap_in[section], 4 * 16)
                pool.tensor_tensor(part, part, factor(1), ALU.mult).then_inc(rope_a, 1)
                pool.tensor_tensor(turned, v, factor(0), ALU.mult).then_inc(rope_a, 1)
                pool.wait_ge(rope_a, 2 * section + 2)
                pool.tensor_tensor(turned, turned, part, ALU.add).then_inc(rope_ok, 1)

            def scale_probs(i):
                pool.wait_ge(weight_ok, i + 1)
                n = 2 if unit_of(i)[1] < 2 else 4
                v = probs[:, i % 2, :].rearrange("p (n k) -> p n k", n=n)
                pool.tensor_tensor(v, v, weight[:, i % 2, 0:n].unsqueeze(2).broadcast_to((P, n, CH // n)),
                                   ALU.mult).then_inc(scaled_ok, 1)

            for section in range(3):
                rope(section)
            for i in range(UNITS):
                scale_probs(i)
                if i in (2, 4, 6, 8):
                    rope(3 + (i - 2) // 2)
            for t in range(TT):
                pool.wait_ge(mom_ok, t + 1)
                pool.tensor_scalar(rstd[:, t, 0:1], moments[:, t, 1:2], LN_EPS, None, ALU.add).then_inc(eps_ok, 1)
                pool.wait_ge(eps_ok, t + 2)
                pool.tensor_tensor(rstd[:, t, 1:2], rstd[:, t, 0:1], rstd[:, t, 2:3], ALU.pow).then_inc(rstd_ok, 1)
                for n in ((0, 1), (2,))[t]:
                    pool.wait_ge(spread, n + 1)
                    if n == 0:
                        wait_piece(pool, ("gb", 0, 0))
                    cols = stretches[n][1]
                    pool.tensor_tensor(total[:, t, cols], total[:, t, cols], bias[:, cols], ALU.add).then_inc(fin_pool, 1)

        @block.scalar
        def _(act):
            def split_first(kt):
                act.wait_ge(x_in[kt], 16)
                act.activation(x_hi[:, kt, :], raw[:, 0, kt * SEQ:(kt + 1) * SEQ], ACT.Copy).then_inc(x_hi_ok, 1)
                act.wait_ge(w_in[kt], 16)
                split_w = act.activation(w_hi[:, kt // 4, kt % 4, :], raw[:, 1 + kt // 4, kt % 4 * CH:(kt % 4 + 1) * CH], ACT.Copy)
                if kt < KT - 1:
                    split_w.then_inc(first_hi, 1)
                else:
                    split_w.then_inc(hi_ok, 4)

            def split(u):
                c, k, j = u // 4, u % 4 // 2, u % 2
                piece = 2 * c + k
                if c == C_NQ:
                    act.wait_ge(nq_in[u % 4], 16)
                else:
                    wait_piece(act, ("w", c, k))
                if piece >= HL:
                    act.wait_ge(group_done, last_use(piece - HL))
                w = width(c)
                n = PIECES.index(("w", c, k))
                src = raw[:, n % RAW, 2 * j * w:2 * (j + 1) * w].rearrange("p (k n) -> p k n", k=2)
                act.activation(w_hi[:, piece % HL, 2 * j:2 * j + 2, 0:w], src, ACT.Copy).then_inc(hi_ok, 1)

            def copy_group(c, t):
                act.wait_ge(group_done, t + 3 if c == C_KV else 4 * c + 2 * t + 2)
                src = acc[t]
                if c == C_KV and t == 0:
                    act.activation(kvc_T[:, :, :].rearrange("p n t -> p (n t)"), src[:, :], ACT.Copy).then_inc(acc_read, 1)
                elif c in (C_KV, C_MK):
                    if (c, t) == (C_MK, 1):
                        act.wait_ge(part_lo, 1)
                    act.activation(keys[:, t, :], src[:, :], ACT.Copy).then_inc(acc_read, 1)
                elif c == C_NQ:
                    act.activation(qraw_T[:, 2 * t:2 * t + 2, :].rearrange("p m t -> p (m t)"), src[:, :],
                                   ACT.Copy, scale=SCALE).then_inc(acc_read, 1)
                elif c == C_MQ:
                    act.wait_ge(part_lo, 2 + t)
                    act.activation(queries[:, t, :], src[:, :], ACT.Copy, scale=SCALE).then_inc(acc_read, 1)
                elif c == C_NV:
                    act.activation(gates[:, t, :], src[:, 2 * KV:NARROW], ACT.Tanh, scale=0.5)
                    act.activation(v_st[:, t, :, 0:HEAD_DIM], src[:, 0:2 * KV].rearrange("p (n d) -> p n d", d=HEAD_DIM),
                                   ACT.Copy).then_inc(v_hi_ok, 1)
                elif c == C_MV:
                    act.activation(vm_st[:, t, :, 0:HEAD_DIM], src[:, :].rearrange("p (n d) -> p n d", d=HEAD_DIM),
                                   ACT.Copy).then_inc(v_hi_ok, 1)
                else:
                    wait_turn(act, "cs" if c == C_NZ else "hv")
                    act.activation(zT[c - C_NZ][:, 2 * t:2 * t + 2, :], src[:, :].rearrange("p (m t) -> p m t", m=2),
                                   ACT.Tanh, scale=0.5).then_inc(z_tanh, 1)

            def exps(i):
                n = 2 if unit_of(i)[1] < 2 else 4
                w = CH // n
                act.wait_ge(max_ok, i + 1)
                if i >= 2:
                    wait_turn(act, f"p{i - 2}")
                    act.wait_ge(weight_ok, i - 1)
                for h in range(n):
                    last = act.activation(probs[:, i % 2, h * w:(h + 1) * w], scores[i % 2][:, h * w:(h + 1) * w], ACT.Exp,
                                          bias=neg_max[:, i % 2, h:h + 1], accum_out=row_sum[:, i % 2, h:h + 1])
                last.then_inc(probs_ok, 1)

            def probs_hi(i):
                wait_turn(act, f"p{i}")
                if i < NSA_UNITS:
                    if i >= 2:
                        act.wait_ge(heads_ok, heads_after(i - 2))
                else:
                    act.wait_ge(heads_ok, heads_after(i - 2 if i % 3 == 1 else i - 1))
                act.activation(pT_hi[:, part_slot(i), :, :].rearrange("p n q -> p (n q)"), turn_bank(f"p{i}")[:, :],
                               ACT.Copy).then_inc(turn_act, 1)

            def section_hi(section):
                act.wait_ge(rope_ok, section + 1)
                c, b = SECTIONS[section]
                v = rotated(section).rearrange("p (m t) -> p m t", m=2)
                if c == C_KV:
                    for g in range(2):
                        for half in range(2):
                            last = act.activation(k_hi[64 * half:64 * half + 64, g, :, :], v[64 * g:64 * g + 64, :, :], ACT.Copy)
                else:
                    st = {C_NQ: q_st, C_MK: km_hi, C_MQ: qm_st}[c]
                    dst = st[0:64, 4 * b:4 * b + 4, :].rearrange("p (m h) t -> p m h t", h=2)
                    for h in range(2):
                        last = act.activation(dst[:, :, h, :], v[64 * h:64 * h + 64, :, :], ACT.Copy)
                last.then_inc(part_hi, 1)

            def heads_start(m):
                act.wait_ge(heads_ok, units_before(m))
                for h in range(2):
                    last = act.activation(o_T[64 * h:64 * h + 64, m, :], heads[m % 2][0:64, h * SEQ:(h + 1) * SEQ], ACT.Copy)
                last.then_inc(heads_hi, 1)

            def y_hi(half, t):
                act.wait_ge(y_ok, 2 * half + t + 1)
                act.wait_ge(scores_ok, 12 if half == 0 else UNITS)
                tok = slice(t * P, (t + 1) * P)
                act.activation(y_parts[half][:, 0:4, tok], o_T[:, 4 * half:4 * half + 4, tok], ACT.Copy).then_inc(y_hi_ok, 1)

            for kt in range(KT):
                split_first(kt)
            for s in range(STEPS):
                i = s - UNIT0
                if 0 <= i - 3 < UNITS:
                    probs_hi(i - 3)
                if 0 <= i - 1 < UNITS:
                    exps(i - 1)
                if s == 10:
                    section_hi(sections_at.index(s))
                if s == 3:
                    copy_group(C_KV, 0)
                if s == 4:
                    copy_group(C_KV, 1)
                elif s % 2 == 0 and s > 4:
                    copy_group((s - 1) // 4, (s - 1) % 4 // 2)
                if s == 15:
                    wait_turn(act, "hT")
                    act.activation(hid[:, :, :, :], turn_bank("hT")[:, :].rearrange("p (a b n) -> p a b n", a=2, b=2),
                                   ACT.Tanh, scale=0.5).then_inc(turn_act, 1)
                if s == 17:
                    act.wait_ge(cmp_shift, 1)
                    act.activation(cmp_p[:, :, :], cmp_p[:, :, :], ACT.Exp).then_inc(cmp_exp, 1)
                if s == 25:
                    wait_turn(act, "cp")
                    act.activation(cmp_pT[:, :], turn_bank("cp")[:, 0:SEQ], ACT.Copy).then_inc(turn_act, 1)
                if s in (19, 22, 25, 27):
                    heads_start((s - 18) // 3)
                if s in sections_at and s != 10:
                    section_hi(sections_at.index(s))
                if s == 21:
                    act.wait_ge(part_lo, 5)
                    act.dma_start(km_hi[64:P, :, :].bitcast(f32), km_hi[0:64, :, :].bitcast(f32)).then_inc(km_in[0], 16)
                    act.dma_start(km_lo[64:P, :, :].bitcast(f32), km_lo[0:64, :, :].bitcast(f32)).then_inc(km_in[1], 16)
                if s in (29, 30):
                    heads_start(s - 25)
                if s == 30:
                    y_hi(0, 0)
                if s == 31:
                    y_hi(0, 1)
                for u in splits_in(s):
                    split(u)
            probs_hi(17)
            copy_group(C_MZ, 1)
            split(4 * C_OB)
            split(4 * C_OB + 1)
            heads_start(6)
            heads_start(7)
            y_hi(1, 0)
            y_hi(1, 1)
            split(4 * C_OB + 2)
            split(4 * C_OB + 3)
            for n, (t, cols) in enumerate(stretches[:3]):
                act.wait_ge(centred, n + 1)
                act.wait_ge(rstd_ok, t + 1)
                act.activation(total[:, t, cols], total[:, t, cols], ACT.Copy, scale=rstd[:, t, 1:2]).then_inc(spread, 1)

        @block.vector
        def _(dve):
            chain = [0]

            def link(instruction):
                chain[0] += 1
                instruction.then_inc(link_done, 1)
                dve.wait_ge(link_done, chain[0])

            def split_first(kt):
                dve.wait_ge(x_hi_ok, kt + 1)
                dve.tensor_tensor(x_lo[:, kt, :], raw[:, 0, kt * SEQ:(kt + 1) * SEQ], x_hi[:, kt, :].bitcast(f32),
                                  ALU.subtract).then_inc(x_lo_ok, 1)
                if kt < KT - 1:
                    dve.wait_ge(first_hi, kt + 1)
                else:
                    dve.wait_ge(hi_ok, 4)
                split_w = dve.tensor_tensor(w_lo[:, kt // 4, kt % 4, :], raw[:, 1 + kt // 4, kt % 4 * CH:(kt % 4 + 1) * CH],
                                            w_hi[:, kt // 4, kt % 4, :].bitcast(f32), ALU.subtract)
                if kt < KT - 1:
                    split_w.then_inc(first_lo, 1)
                else:
                    split_w.then_inc(lo_ok, 4)

            def split(u):
                c, k, j = u // 4, u % 4 // 2, u % 2
                piece = 2 * c + k
                w = width(c)
                n = PIECES.index(("w", c, k))
                dve.wait_ge(hi_ok, u + 1)
                src = raw[:, n % RAW, 2 * j * w:2 * (j + 1) * w].rearrange("p (k n) -> p k n", k=2)
                at = (slice(None), piece % HL, slice(2 * j, 2 * j + 2), slice(0, w))
                dve.tensor_tensor(w_lo[at], src, w_hi[at].bitcast(f32), ALU.subtract).then_inc(lo_ok, 1)

            def values_lo(c, t):
                dve.wait_ge(v_hi_ok, 2 * (c == C_MV) + t + 1)
                st = v_st if c == C_NV else vm_st
                n = 2 * GROUPS if c == C_NV else 8
                dve.tensor_tensor(st[:, t, :, HEAD_DIM:P], acc[t][:, 0:n * HEAD_DIM].rearrange("p (n d) -> p n d", d=HEAD_DIM),
                                  st[:, t, :, 0:HEAD_DIM].bitcast(f32), ALU.subtract).then_inc(v_ok, 1)

            def silu_out(c, b):
                dve.wait_ge(z_tanh, 2 * (c - C_NZ) + b + 1)
                part = zT[c - C_NZ][:, 2 * b:2 * b + 2, :]
                dve.scalar_tensor_tensor(part, part, 1.0, acc[b][:, :].rearrange("p (m t) -> p m t", m=2),
                                         ALU.add, ALU.mult).then_inc(z_read, 1)

            def maxima(i):
                dve.wait_ge(scores_ok, i + 1)
                if i >= 2:
                    dve.wait_ge(probs_ok, i - 1)
                n = 2 if unit_of(i)[1] < 2 else 4
                dve.tensor_reduce(neg_max[:, i % 2, 0:n], scores[i % 2][:, :].rearrange("p (n k) -> p n k", n=n),
                                  AX.X, ALU.max, negate=True).then_inc(max_ok, 1)

            def probs_lo(i):
                dve.wait_ge(turn_act, act_turns(f"p{i}"))
                slot = part_slot(i)
                dve.tensor_tensor(pT_lo[:, slot, :, :].rearrange("p n q -> p (n q)"), turn_bank(f"p{i}")[:, :],
                                  pT_hi[:, slot, :, :].bitcast(f32).rearrange("p n q -> p (n q)"),
                                  ALU.subtract).then_inc(turn_dve, 1)

            def weights(i):
                g, kind = unit_of(i)
                n = 2 if kind < 2 else 4
                dve.wait_ge(probs_ok, i + 1)
                if i >= 2:
                    dve.wait_ge(scaled_ok, i - 1)
                if g >= 4:
                    dve.reciprocal(weight[:, i % 2, 0:n], row_sum[:, i % 2, 0:n]).then_inc(weight_ok, 1)
                    return
                link(dve.reciprocal(inverse[:, 0:n], row_sum[:, i % 2, 0:n]))
                if kind < 2:
                    gate = gates[:, 1, (1 + kind) * 8 + 2 * g:(1 + kind) * 8 + 2 * g + 2]
                    dve.tensor_tensor(weight[:, i % 2, 0:2], inverse[:, 0:2], gate, ALU.mult).then_inc(weight_ok, 1)
                else:
                    gate = gates[:, 0, 8:24].rearrange("p (b h) -> p h b", b=2)[:, 2 * g:2 * g + 2, :]
                    dve.tensor_tensor(weight[:, i % 2, :].rearrange("p (h b) -> p h b", h=2),
                                      inverse[:, :].rearrange("p (h b) -> p h b", h=2), gate, ALU.mult).then_inc(weight_ok, 1)

            def section_lo(section):
                dve.wait_ge(part_hi, section + 1)
                c, b = SECTIONS[section]
                v = rotated(section).rearrange("p (m t) -> p m t", m=2)
                if c == C_KV:
                    for g in range(2):
                        for half in range(2):
                            rows = slice(64 * half, 64 * half + 64)
                            last = dve.tensor_tensor(k_lo[rows, g, :, :], v[64 * g:64 * g + 64, :, :],
                                                     k_hi[rows, g, :, :].bitcast(f32), ALU.subtract)
                else:
                    st = {C_NQ: q_st, C_MK: km_hi, C_MQ: qm_st}[c]
                    group = lambda x: x[:, 4 * b:4 * b + 4, :].rearrange("p (m h) t -> p m h t", h=2)
                    hi, lo = group(st[0:64]).bitcast(f32), group(km_lo[0:64] if c == C_MK else st[64:P])
                    for h in range(2):
                        last = dve.tensor_tensor(lo[:, :, h, :], v[64 * h:64 * h + 64, :, :], hi[:, :, h, :], ALU.subtract)
                last.then_inc(part_lo, 1)

            def heads_add(m):
                dve.wait_ge(heads_hi, m + 1)
                for h in range(2):
                    rows = slice(64 * h, 64 * h + 64)
                    last = dve.tensor_tensor(o_T[rows, m, :], heads[m % 2][64:P, h * SEQ:(h + 1) * SEQ], o_T[rows, m, :], ALU.add)
                last.then_inc(heads_read, 1)

            def compressed_add(half):
                wait_turn(dve, f"oc{half}")
                dve.wait_ge(heads_read, 2 * half + 2)
                part = o_T[:, 2 * half:2 * half + 2, :].rearrange("p m t -> p (m t)")
                dve.tensor_tensor(part, turn_bank(f"oc{half}")[:, :], part, ALU.add).then_inc(turn_dve, 1)

            def gate_y(half, t):
                if half == 0:
                    dve.wait_ge(turn_dve, dve_turns("oc1"))
                else:
                    dve.wait_ge(heads_read, 8)
                dve.wait_ge(z_read, 2 * half + 2)
                tok = slice(t * P, (t + 1) * P)
                part = o_T[:, 4 * half:4 * half + 4, tok]
                dve.scalar_tensor_tensor(part, part, 0.5, zT[half][:, :, tok], ALU.mult, ALU.mult).then_inc(y_ok, 1)

            def y_lo(half, t):
                dve.wait_ge(y_hi_ok, 2 * half + t + 1)
                tok = slice(t * P, (t + 1) * P)
                dve.tensor_tensor(y_parts[half][:, 4:8, tok], o_T[:, 4 * half:4 * half + 4, tok],
                                  y_parts[half][:, 0:4, tok].bitcast(f32), ALU.subtract).then_inc(y_lo_ok, 1)

            def pack(kind):
                for g in range(GROUPS):
                    rows = slice(64 * g, 64 * g + 64)
                    src = kvc_T[rows, kind, :].rearrange("p (c w) -> p c w", w=CMP_STRIDE)
                    for parity in range(2):
                        for half in range(2):
                            n = CKT // 2
                            v = src[:, half:half + NCMP, parity::2].rearrange("p c k -> p k c")
                            term = pos_sb[rows, kind, parity, half * n:(half + 1) * n].unsqueeze(2).broadcast_to((64, n, NCMP))
                            dve.tensor_tensor(cmp_in[64 * parity:64 * parity + 64, kind, half * n:(half + 1) * n,
                                                     g * CPAD:g * CPAD + NCMP], v, term, ALU.add).then_inc(packed, 1)

            for kt in range(KT):
                split_first(kt)
            for s in range(STEPS):
                i = s - UNIT0
                if 0 <= i - 1 < UNITS:
                    maxima(i - 1)
                if 0 <= i - 3 < UNITS:
                    probs_lo(i - 3)
                if s == 12:
                    section_lo(sections_at.index(s))
                for u in low_splits_in(s):
                    split(u)
                if 0 <= i - 1 < UNITS:
                    weights(i - 1)
                if s % 2 == 0 and (s - 1) // 4 in (C_NV, C_MV):
                    values_lo((s - 1) // 4, (s - 1) % 4 // 2)
                if s % 2 == 0 and (s - 1) // 4 >= C_NZ:
                    silu_out((s - 1) // 4, (s - 1) % 4 // 2)
                if s == 6:
                    dve.wait_ge(acc_read, 1)
                    dve.wait_ge(pos_in, 16)
                    dve.wait_ge(zero_ok, 1)
                    pack(0)
                if s == 7:
                    dve.wait_ge(k_in, 16)
                    dve.wait_ge(mask_in, 16)
                    dve.tensor_copy(ident_bf[:, :], ident)
                    dve.tensor_copy(causal_bf[:, :], masks[:, 0:P])
                    dve.tensor_copy(cmask_bf[:, :, :], masks[:, P:3 * P].rearrange("p (t n) -> p t n", t=TT)).then_inc(bf_ok, 1)
                if s == 8:
                    pack(1)
                if s == 12:
                    link(dve.tensor_scalar(gates[:, :, :], gates[:, :, :], 1.0, 0.5, ALU.add, ALU.mult))
                if s == 13:
                    wait_turn(dve, "hk")
                    dve.tensor_copy(hid_parts[:, 0, :], turn_bank("hk")[:, 0:CMP_HIDDEN]).then_inc(turn_dve, 1)
                if s == 14:
                    wait_turn(dve, "hv")
                    dve.tensor_copy(hid_parts[:, 1, :], turn_bank("hv")[:, 0:CMP_HIDDEN]).then_inc(turn_dve, 1)
                if s == 15:
                    dve.wait_ge(turn_act, act_turns("hT"))
                    dve.scalar_tensor_tensor(hid[:, :, :, :].rearrange("p a b n -> p (a b n)"),
                                             hid[:, :, :, :].rearrange("p a b n -> p (a b n)"), 1.0,
                                             turn_bank("hT")[:, :], ALU.add, ALU.mult).then_inc(turn_dve, 1)
                if s == 16:
                    wait_turn(dve, "kcvc")
                    b = turn_bank("kcvc")
                    keys = b[:, 0:GROUPS * CPAD].rearrange("p (g c) -> p g c", g=GROUPS)
                    dve.wait_ge(zero_ok, 2)
                    dve.tensor_scalar(kc_B[0:64, :, 0:CPAD], keys[0:64], 0.5, None, ALU.mult)
                    dve.tensor_scalar(kc_B[64:P, :, CPAD:2 * CPAD], keys[64:P], 0.5, None, ALU.mult)
                    dve.tensor_tensor(vc_B[:, :, :].rearrange("p m (h d) -> p (m h) d", d=HEAD_DIM),
                                      b[:, 64:P].unsqueeze(1).broadcast_to((P, 8, HEAD_DIM)),
                                      const(K_BLOCK).unsqueeze(2).broadcast_to((P, 8, HEAD_DIM)), ALU.mult).then_inc(turn_dve, 1)
                if s == 17:
                    wait_turn(dve, "cs")
                    b = turn_bank("cs")[:, 0:TT * P].rearrange("p (n c) -> p n c", c=CPAD)
                    stat = lambda n: cmp_stat[:, n, :, :].rearrange("p t h -> p (t h)")
                    wide = lambda n: stat(n).unsqueeze(2).broadcast_to((P, TT * 8, CPAD))
                    e = cmp_p[:, :, :].rearrange("p t (h c) -> p (t h) c", c=CPAD)
                    link(dve.tensor_reduce(stat(0), b, AX.X, ALU.max, negate=True))
                    dve.tensor_tensor(e, b, wide(0), ALU.add).then_inc(turn_dve, 1)
                    dve.wait_ge(turn_dve, dve_turns("cs"))
                    dve.memset(inverse[:, 0:1], 0.0).then_inc(cmp_shift, 1)
                if s == 18:
                    dve.wait_ge(cmp_exp, 1)
                    for t2 in range(TT):
                        e2 = cmp_p[:, t2, :].rearrange("p (h c) -> p h c", c=CPAD)
                        last = dve.tensor_tensor(e2, e2, const(K_CVALID)[:, t2 * CPAD:(t2 + 1) * CPAD].unsqueeze(1)
                                                 .broadcast_to((P, 8, CPAD)), ALU.mult)
                    link(last)
                    link(dve.tensor_reduce(stat(1), e, AX.X, ALU.add))
                    link(dve.tensor_scalar(stat(1), stat(1), 0.5, None, ALU.max))
                    link(dve.reciprocal(stat(2), stat(1)))
                    link(dve.tensor_tensor(cmp_stat[:, 2, :, :], cmp_stat[:, 2, :, :], gates[:, :, 0:8], ALU.mult))
                    dve.tensor_tensor(e, e, wide(2), ALU.mult).then_inc(cmp_pok, 1)
                if s in (19, 22, 25, 27):
                    heads_add((s - 18) // 3)
                if s in sections_at and s != 12:
                    section_lo(sections_at.index(s))
                if s == 27:
                    compressed_add(0)
                if s == 29:
                    compressed_add(1)
                    gate_y(0, 0)
                if s in (29, 30):
                    heads_add(s - 25)
                if s == 30:
                    gate_y(0, 1)
                    y_lo(0, 0)
                if s == 31:
                    y_lo(0, 1)
                if s % 4 == 3:
                    split(s + 3)
            probs_lo(17)
            silu_out(C_MZ, 1)
            split(4 * C_OB - 1)
            split(4 * C_OB)
            split(4 * C_OB + 1)
            heads_add(6)
            heads_add(7)
            gate_y(1, 0)
            gate_y(1, 1)
            y_lo(1, 0)
            y_lo(1, 1)
            split(4 * C_OB + 2)
            split(4 * C_OB + 3)
            wait_piece(dve, ("res", 0, 0))
            wait_piece(dve, ("gb", 0, 0))

            def centre(n):
                t, cols = stretches[n]
                return dve.scalar_tensor_tensor(total[:, t, cols], total[:, t, cols], moments[:, t, 0:1], gain[:, cols],
                                                ALU.subtract, ALU.mult)

            def residual(n):
                t, col, w = OUT_PARTS[n]
                dve.wait_ge(out_ok, n + 1)
                dve.scalar_tensor_tensor(total[:, t, col:col + w], x_tok[:, t, col:col + w], ALPHA,
                                         out_bank[n][:, 0:w], ALU.mult, ALU.add).then_inc(total_ok, 1)

            def part_stats(n):
                t, col, w = OUT_PARTS[n]
                size = (CH, CH // 2)[t]
                dve.wait_ge(total_ok, n + 1)
                for at in range(col, col + w, size):
                    last = dve.bn_stats(stats[:, t, at // size, :], total[:, t, at:at + size])
                last.then_inc(stats_ok, 1)

            def tile_moments(t):
                dve.wait_ge(stats_ok, (2, 5)[t])
                dve.bn_aggr(moments[:, t, :], stats[:, t, 0:(2, 4)[t], :].rearrange("p n s -> p (n s)")).then_inc(mom_ok, 1)

            residual(0)
            part_stats(0)
            residual(1)
            part_stats(1)
            tile_moments(0)
            dve.wait_ge(mom_ok, 1)
            centre(0).then_inc(centred, 1)
            centre(1).then_inc(centred, 1)
            residual(2)
            part_stats(2)
            residual(3)
            part_stats(3)
            residual(4)
            part_stats(4)
            tile_moments(1)
            dve.wait_ge(mom_ok, 2)
            centre(2).then_inc(centred, 1)
            for n in (3, 4):
                t, cols = stretches[n]
                centre(n).then_inc(centred, 1)
                dve.wait_ge(centred, n + 1)
                dve.wait_ge(rstd_ok, TT)
                dve.scalar_tensor_tensor(total[:, t, cols], total[:, t, cols], rstd[:, t, 1:2], bias[:, cols],
                                         ALU.mult, ALU.add).then_inc(fin_dve, 1)

        @block.tensor
        def _(pe):
            def project_tile(c, t, kt):
                w = width(c)
                piece, j, tok = (2 * c + kt // 4) % HL, kt % 4, slice(t * P, (t + 1) * P)
                pe.matmul(acc[t][:, 0:w], x_hi[:, kt, tok], w_hi[:, piece, j, 0:w], start=(kt == 0), stop=False)
                pe.matmul(acc[t][:, 0:w], x_hi[:, kt, tok], w_lo[:, piece, j, 0:w], start=False, stop=False)
                return pe.matmul(acc[t][:, 0:w], x_lo[:, kt, tok], w_hi[:, piece, j, 0:w], start=False, stop=(kt == KT - 1))

            def project_first(s):
                for kt in ((2 * s, 2 * s + 1) if s < 2 else range(4, 8)):
                    banks = range(2) if s < 2 else (s - 2,)

                    def part(b, m, x, w):
                        return pe.matmul(acc[b][:, m * SEQ:(m + 1) * SEQ], w[:, kt // 4, kt % 4, (2 * b + m) * P:(2 * b + m + 1) * P],
                                         x[:, kt, :], start=(kt == 0 and m == 0 and x is x_hi and w is w_hi),
                                         stop=(kt == KT - 1 and m == 1 and x is x_lo), skip_group_check=True)

                    if s < 3:
                        if kt < KT - 1:
                            pe.wait_ge(first_hi, kt + 1)
                        else:
                            pe.wait_ge(hi_ok, 4)
                    for b in banks:
                        for m in range(2):
                            part(b, m, x_hi, w_hi)
                    if s < 3:
                        pe.wait_ge(x_lo_ok, kt + 1)
                        if kt < KT - 1:
                            pe.wait_ge(first_lo, kt + 1)
                        else:
                            pe.wait_ge(lo_ok, 4)
                    for b in banks:
                        for m in range(2):
                            part(b, m, x_hi, w_lo)
                            last = part(b, m, x_lo, w_hi)
                last.then_inc(group_done, 1)

            def project_transposed_tile(c, b, kt):
                piece, j = (2 * c + kt // 4) % HL, kt % 4
                for m in range(2):
                    dst, cols = acc[b][:, m * SEQ:(m + 1) * SEQ], slice((2 * b + m) * P, (2 * b + m + 1) * P)
                    pe.matmul(dst, w_hi[:, piece, j, cols], x_hi[:, kt, :], start=(kt == 0 and m == 0), stop=False,
                              skip_group_check=True)
                    pe.matmul(dst, w_hi[:, piece, j, cols], x_lo[:, kt, :], start=False, stop=False, skip_group_check=True)
                    last = pe.matmul(dst, w_lo[:, piece, j, cols], x_hi[:, kt, :], start=False,
                                     stop=(kt == KT - 1 and m == 1), skip_group_check=True)
                return last

            def project(s):
                c, t, k = s // 4, s % 4 // 2, s % 2
                n = 2 * c + t
                if k == 0:
                    old = (n - 2) // 2
                    if old in (C_NV, C_MV):
                        pe.wait_ge(v_ok, 2 * (old == C_MV) + t + 1)
                    elif old == C_NZ:
                        pe.wait_ge(z_read, t + 1)
                    else:
                        pe.wait_ge(acc_read, sections_before(old) + t + 1)
                for kt in range(4 * k, 4 * k + 4):
                    if t == 0 and kt % 2 == 0:
                        pe.wait_ge(lo_ok, 4 * c + kt // 2 + 1)
                    last = (project_transposed_tile if c in TRANSPOSED else project_tile)(c, t, kt)
                last.then_inc(group_done, 1)

            def transposes(name, blocks, n=4):
                wait_turn_free(pe, name)
                for m in range(n):
                    last = pe.transpose(turn_bank(name)[:, m * P:(m + 1) * P], blocks(m), ident)
                last.then_inc(turn_full, 1)

            def unit_scores(i):
                g, kind = unit_of(i)
                if i >= 2:
                    pe.wait_ge(probs_ok, i - 1)
                bank = scores[i % 2]
                q_tokens = slice(P, SEQ) if kind < 2 else slice(0, P)
                if g < 4:
                    work = [(q_st[:, 2 * g + h, q_tokens],
                             [k[:, g // 2, kind, :] if kind < 2 else k[:, g // 2, :, 0:P] for k in (k_hi, k_lo)])
                            for h in range(2)]
                else:
                    first = 4 * (g - 4) + (2 * kind if kind < 2 else 0)
                    work = [(qm_st[:, head, q_tokens], [k[:, head, 0:SEQ if kind < 2 else P] for k in (km_hi, km_lo)])
                            for head in range(first, first + (2 if kind < 2 else 4))]
                w = CH // len(work)
                for n, (q, parts) in enumerate(work):
                    for part, keys in enumerate(parts):
                        dst = bank[:, n * w:(n + 1) * w]
                        if len(keys.shape) == 3:
                            dst = dst.rearrange("p (b k) -> p b k", b=2)
                        pe.matmul(dst, q, keys, start=(n == 0 and part == 0), stop=False, skip_group_check=True)
                tiles = bank[:, :].rearrange("p (n k) -> p n k", k=P)
                causal = causal_bf[:, :].unsqueeze(1).broadcast_to((P, 2, P))
                if kind < 2:
                    last = pe.matmul(tiles[:, 1::2, :], ident_bf[:, :], causal, start=False, stop=True,
                                     skip_group_check=True)
                else:
                    for n in range(2):
                        last = pe.matmul(tiles[:, 2 * n:2 * n + 2, :], ident_bf[:, :], causal, start=False,
                                         stop=(n == 1), skip_group_check=True)
                last.then_inc(scores_ok, 1)

            def unit_turn(i):
                pe.wait_ge(scaled_ok, i + 1)
                transposes(f"p{i}", lambda m: probs[:, i % 2, m * P:(m + 1) * P])

            def unit_heads(i):
                g, kind = unit_of(i)
                pe.wait_ge(turn_dve, dve_turns(f"p{i}"))
                if g < 4:
                    if kind == 0 and g >= 2:
                        pe.wait_ge(heads_read, g - 1)
                    out_h = heads[g % 2][:, :].rearrange("p (h q) -> p h q", h=2)
                    passes = [(part, x) for x in range(2) for part in (pT_hi, pT_lo)]
                    for n, (part, x) in enumerate(passes):
                        p4 = part[:, i % 2, :, :].rearrange("p (h x) q -> p h x q", h=2)[:, :, x, :]
                        branch, tile = (kind, x) if kind < 2 else (x, 0)
                        last = pe.matmul(out_h[:, :, P:SEQ] if kind < 2 else out_h[:, :, 0:P],
                                         v_st[:, tile, branch * GROUPS + g // 2, :], p4,
                                         start=(n == 0 and kind != 1), stop=(n == 3 and kind != 0), skip_group_check=True)
                elif i % 3 > 0:
                    second = i % 3 - 1
                    pair = 2 * (g - 4) + second
                    pe.wait_ge(heads_read, pair + 3)
                    for h in range(2):
                        at, first, own = h * SEQ, 2 * second + h, 4 * part_slot(3 * g) + 2 * h
                        for kt in range(2):
                            for n, part in enumerate((pT_hi, pT_lo)):
                                blocks = part[:, :, :, :].rearrange("p s n q -> p (s n) q")
                                if kt == 0:
                                    dst, p = heads[pair % 2][:, at:at + SEQ], blocks[:, first:own + 1:own - first, :]
                                else:
                                    dst, p = heads[pair % 2][:, at + P:at + SEQ], blocks[:, own + 1, :]
                                last = pe.matmul(dst, vm_st[:, kt, 2 * pair + h, :], p, start=(h == 0 and kt == 0 and n == 0),
                                                 stop=(h == 1 and kt == 1 and n == 1), skip_group_check=True)
                if i < NSA_UNITS or i % 3 > 0:
                    last.then_inc(heads_ok, 1)

            def hidden(kind, name):
                wait_turn_free(pe, name)
                pe.wait_ge(packed, 8 * kind + 8)
                for i in range(CKT):
                    if i % 8 == 0:
                        n = PIECES.index((("fk", "fv")[kind], kind, i // 8))
                        wait_piece(pe, PIECES[n])
                    j = i % 4
                    w = raw[:, n % RAW, (i % 8) * CMP_HIDDEN:(i % 8 + 1) * CMP_HIDDEN]
                    last = pe.matmul(turn_bank(name)[32 * j:32 * j + 32, 0:CMP_HIDDEN], cmp_in[:, kind, i, :], w,
                                     start=(i < 4), stop=(i >= CKT - 4))
                    if i == CKT // 2 - 1:
                        last.then_inc(hid_read, 1)
                last.then_inc(turn_full, 1)

            def compressed_heads(half):
                wait_turn_free(pe, f"oc{half}")
                pe.wait_ge(turn_act, act_turns("cp"))
                for m in range(2):
                    last = pe.matmul(turn_bank(f"oc{half}")[:, m * SEQ:(m + 1) * SEQ], vc_B[:, 2 * half + m, :], cmp_pT[:, :],
                                     start=True, stop=True)
                last.then_inc(turn_full, 1)

            pe.wait_ge(idle_ok, 1)
            for n in range(WARM_UP):
                pe.matmul(heads[0][:, 0:P], hid_parts[:, 0, 0:P], hid_parts[:, 0, 0:P], start=True, stop=True)
            for s in range(STEPS):
                i = s - UNIT0
                if s < 4:
                    project_first(s)
                else:
                    project(s)
                if i == 3:
                    pe.wait_ge(v_ok, 2)
                if i == 6:
                    pe.wait_ge(part_lo, 3)
                if i == 12:
                    pe.wait_ge(part_lo, 6)
                    pe.wait_ge(km_in[0], 16)
                    pe.wait_ge(km_in[1], 16)
                if i == 15:
                    pe.wait_ge(part_lo, 7)
                    pe.wait_ge(v_ok, 4)
                if s == 12:
                    hidden(0, "hk")
                if i == 0:
                    pe.wait_ge(bf_ok, 1)
                    pe.wait_ge(part_lo, 2)
                if 0 <= i < UNITS:
                    unit_scores(i)
                if 0 <= i - 2 < UNITS:
                    unit_turn(i - 2)
                if 0 <= i - 3 < UNITS:
                    unit_heads(i - 3)
                if s == 13:
                    hidden(1, "hv")
                if s == 14:
                    wait_turn_free(pe, "hT")
                    pe.wait_ge(turn_dve, dve_turns("hv"))
                    pe.wait_ge(k_in, 16)
                    pe.wait_ge(b1_in, 16)
                    pe.wait_ge(zero_ok, 3)
                    for kind in range(2):
                        for half in range(2):
                            cols = slice(half * P, (half + 1) * P)
                            dst = turn_bank("hT")[:, (2 * kind + half) * P:(2 * kind + half + 1) * P]
                            pe.matmul(dst, hid_parts[:, kind, cols], const(K_SEL), start=True, stop=False)
                            last = pe.matmul(dst, b1_sb[:, kind, cols], ones_sb[:, :], start=False, stop=True)
                    last.then_inc(turn_full, 1)
                if s == 15:
                    wait_turn_free(pe, "kcvc")
                    pe.wait_ge(turn_dve, dve_turns("hT"))
                    pe.wait_ge(w2k_in, 16)
                    pe.wait_ge(w2v_in, 16)
                    for copy in range(2):
                        rows = slice(64 * copy, 64 * copy + 64)
                        for half in range(2):
                            blocks = hid[:, 0, half, :].rearrange("p (g n) -> p g n", g=GROUPS)[:, :, 0:CPAD]
                            pe.matmul(turn_bank("kcvc")[rows, 0:GROUPS * CPAD].rearrange("p (g n) -> p g n", g=GROUPS),
                                      w2k_sb[:, half, :], blocks, start=(half == 0), stop=(half == 1))
                    for half in range(2):
                        last = pe.matmul(turn_bank("kcvc")[:, 64:P], hid[:, 1, half, :], w2v_sb[:, half, :],
                                         start=(half == 0), stop=(half == 1))
                    last.then_inc(turn_full, 1)
                if s == 16:
                    wait_turn_free(pe, "cs")
                    pe.wait_ge(turn_dve, dve_turns("kcvc"))
                    for t in range(TT):
                        for m in range(4):
                            at = t * P + m * 2 * CPAD
                            pe.matmul(turn_bank("cs")[:, at:at + 2 * CPAD], qraw_T[:, m, t * P:(t + 1) * P],
                                      kc_B[:, m // 2, :], start=(t == 0 and m == 0), stop=False, skip_group_check=True)
                    last = pe.matmul(turn_bank("cs")[:, 0:TT * P], ident_bf[:, :], cmask_bf[:, :, :].rearrange("p t n -> p (t n)"),
                                     start=False, stop=True, skip_group_check=True)
                    last.then_inc(turn_full, 1)
                if s == 24:
                    pe.wait_ge(cmp_pok, 1)
                    transposes("cp", lambda m: cmp_p[:, m, :], TT)
                if s == 26:
                    compressed_heads(0)
                if s == 28:
                    compressed_heads(1)

            def out_half(c, part):
                t, col, w = OUT_PARTS[part]
                first, cols = 2 * (c - C_OA) + col // CH, slice(col % CH, col % CH + w)
                parts, bank, tok = y_parts[c - C_OA], out_bank[part][:, 0:w], slice(t * P, (t + 1) * P)
                piece = (2 * C_OA + first) % HL
                for j in range(4):
                    if j % 2 == 0:
                        pe.wait_ge(lo_ok, 4 * C_OA + 2 * first + j // 2 + 1)
                    pe.matmul(bank, parts[:, j, tok], w_hi[:, piece, j, cols], start=(c == C_OA and j == 0), stop=False)
                    pe.matmul(bank, parts[:, j, tok], w_lo[:, piece, j, cols], start=False, stop=False)
                    last = pe.matmul(bank, parts[:, 4 + j, tok], w_hi[:, piece, j, cols], start=False,
                                     stop=(c == C_OB and j == 3))
                last.then_inc(group_done if c == C_OA else out_ok, 1)

            pe.wait_ge(z_read, 3)
            pe.wait_ge(y_lo_ok, 1)
            out_half(C_OA, 0)
            unit_heads(17)
            pe.wait_ge(z_read, 4)
            pe.wait_ge(probs_ok, UNITS)
            pe.wait_ge(y_lo_ok, 2)
            out_half(C_OA, 2)
            out_half(C_OA, 1)
            out_half(C_OA, 3)
            pe.wait_ge(turn_dve, dve_turns("p16"))
            out_half(C_OA, 4)
            for part, (t, _, _) in enumerate(OUT_PARTS):
                pe.wait_ge(y_lo_ok, 3 + t)
                out_half(C_OB, part)


def last_use(piece):
    c, k = piece // 2, piece % 2
    if c == C_KV:
        return 2 * k + 2
    if c < C_OA:
        return 4 * c + 2 + k + 1
    return STEPS + (2, len(OUT_PARTS))[k]


def splits_in(s):
    c = s // 4 + 1
    if c == C_MQ:
        return {0: [], 1: [], 2: [4 * c, 4 * c + 1], 3: [4 * c + 2, 4 * c + 3]}[s % 4]
    return {0: [4 * c], 1: [4 * c + 1], 2: [], 3: [4 * c + 2, 4 * c + 3]}[s % 4]


def low_splits_in(s):
    c = s // 4 + 1
    if c == C_MQ:
        return {0: [4 * c - 1], 1: [], 2: [], 3: [4 * c, 4 * c + 1]}[s % 4]
    return {0: [4 * c - 1] if s else [], 1: [4 * c], 2: [4 * c + 1], 3: []}[s % 4]


def kernel(x, w_in, cmp_pos_k, cmp_w1_k, cmp_b1_k, cmp_w2_k,
           cmp_pos_v, cmp_w1_v, cmp_b1_v, cmp_w2_v, w_out, ln_gain, ln_bias):
    import concourse.bacc as bacc
    from concourse.bass_utils import run_bass_kernel_spmd

    a = lambda v: np.asarray(v)
    x, w, wo = a(x)[0], a(w_in)[0], a(w_out)[0]
    sizes = [D_NSA] + [KV] * 6 + [GATES, D_NSA] + [D_MOBA] * 4
    at = np.cumsum([0] + sizes)
    q, kc, vc, ks, vs, kw, vw, ga, z, mq, mk, mv, mz = (w[:, at[n]:at[n + 1]] for n in range(13))

    def pieces(m):
        return m.reshape(2, 4, P, -1).transpose(0, 2, 1, 3).reshape(2, P, -1)

    ga = ga.reshape(D_MODEL, GROUPS * REPS, 3).transpose(0, 2, 1).reshape(D_MODEL, GATES)

    def out_pieces(m):
        return m.reshape(4, P, 2, CH).transpose(2, 1, 0, 3).reshape(2, P, 4 * CH)

    def ordered(m):
        return m.reshape(len(m), -1, HEAD_DIM)[:, :, HEAD_ORDER].reshape(m.shape)

    chunks = [np.concatenate([kc, vc, ordered(ks), ordered(kw)], 1), ordered(q), ordered(mk), ordered(mq), mv, z, mz]
    w_full = np.concatenate([pieces(m) for m in chunks] + [out_pieces(wo[:D_NSA]), out_pieces(wo[D_NSA:])])
    w_nv = pieces(np.concatenate([vs, vw, ga], 1))
    w1 = np.stack([a(m)[0].reshape(2, CKT // 2, P, CMP_HIDDEN).transpose(0, 2, 1, 3).reshape(2, P, PIECE)
                   for m in (cmp_w1_k, cmp_w1_v)])
    pos = np.stack([a(m)[0].reshape(CKT, 2, HEAD_DIM).transpose(2, 1, 0) for m in (cmp_pos_k, cmp_pos_v)], 1)
    pos = np.concatenate([pos, pos], 0)
    b1 = np.stack([a(cmp_b1_k)[0], a(cmp_b1_v)[0]])[None]
    w2k = ordered(a(cmp_w2_k)[0]).reshape(2, P, HEAD_DIM).transpose(1, 0, 2)
    w2v = a(cmp_w2_v)[0].reshape(2, P, HEAD_DIM).transpose(1, 0, 2)
    xT = x.T.reshape(KT, P, SEQ).transpose(1, 0, 2).reshape(P, KT * SEQ)
    x_res = x.reshape(TT, P, D_MODEL).transpose(1, 0, 2).reshape(P, TT * D_MODEL)
    gain_bias = np.concatenate([a(ln_gain)[0], a(ln_bias)[0]])

    nc = bacc.Bacc("TRN2", target_bir_lowering=False, num_devices=1)
    arrays, args = {}, []
    for name, v in (("xT", xT), ("w_full", w_full), ("w_nv", w_nv), ("w1", w1), ("kmat", constants()), ("ropeT", rope_rows()), ("pos", pos),
                    ("b1", b1), ("w2k", w2k), ("w2v", w2v), ("x_res", x_res), ("gain_bias", gain_bias)):
        v = np.ascontiguousarray(v)
        arrays[f"in_{name}"] = v
        args.append(nc.dram_tensor(f"in_{name}", v.shape, mybir.dt.from_np(v.dtype), kind="ExternalInput").ap())
    out = nc.dram_tensor("out_0", (SEQ, D_MODEL), mybir.dt.float32, kind="ExternalOutput").ap()
    build(nc, *args, out)
    r = run_bass_kernel_spmd(nc, [arrays], core_ids=[0])
    return r.results[0]["out_0"].reshape(1, SEQ, D_MODEL)
```
